# Optimizing a Trainium2 kernel written in Bass

```python
import math
import jax, jax.numpy as jnp
from jax import lax
import numpy as np

D_MODEL = 1024
BATCH = 1
SEQ = 512
DEPTH = 2

HEAD_DIM = 64
A_GROUPS = ((128, 1), (512, 4), (2048, 16))
A_HEADS_PER_GROUP = 4
A_N_GROUPS = len(A_GROUPS)
A_WIDTH = A_N_GROUPS * A_HEADS_PER_GROUP * HEAD_DIM
A_OUT = A_HEADS_PER_GROUP * HEAD_DIM
BLK = 128
B_CHUNK = 128
B_GROUPS = 4
B_WIDTH = 512
B_GROUP_DIM = B_WIDTH // B_GROUPS
C_WINDOWS = (2, 4, 8, 16)
C_GROUPS = len(C_WINDOWS)
C_WIDTH = 512
C_GROUP_DIM = C_WIDTH // C_GROUPS
N_BRANCH = 3
D_FF = 2816
EPS = 1e-6

Q_OFF = 0
K_OFF = Q_OFF + A_WIDTH
V_OFF = K_OFF + A_WIDTH
UB_OFF = V_OFF + A_WIDTH
VB_OFF = UB_OFF + B_WIDTH
C_OFF = VB_OFF + B_WIDTH
G_OFF = C_OFF + C_WIDTH
IN_WIDTH = G_OFF + N_BRANCH * D_MODEL

kernel_name = "hybrid_dilated_gmlp_pool_macaron"

def rms_norm(x, g):
    xf = x.astype(jnp.float32)
    y = xf * lax.rsqrt(jnp.mean(xf * xf, axis=-1, keepdims=True) + EPS)
    return (y * g.astype(jnp.float32)).astype(x.dtype)

def layer_norm(x, g, b):
    xf = x.astype(jnp.float32)
    mu = jnp.mean(xf, axis=-1, keepdims=True)
    xc = xf - mu
    y = xc * lax.rsqrt(jnp.mean(xc * xc, axis=-1, keepdims=True) + EPS)
    return (y * g.astype(jnp.float32) + b.astype(jnp.float32)).astype(x.dtype)

def swiglu(h, w_gate, w_up, w_down):
    return (jax.nn.silu(h @ w_gate) * (h @ w_up)) @ w_down

def dilated_window_attention(q, k, v, window, dil):
    Bn, S, H, Dh = q.shape
    span = window // dil
    unit = dil * BLK
    S_pad = -(-S // unit) * unit
    L = S_pad // dil
    nb = L // BLK

    def to_strided(t):
        t = jnp.pad(t, ((0, 0), (0, S_pad - S), (0, 0), (0, 0)))
        t = t.reshape(Bn, L, dil, H, Dh).transpose(0, 2, 3, 1, 4)
        return t.reshape(Bn, dil, H, nb, BLK, Dh)

    qs, ks, vs = to_strided(q), to_strided(k), to_strided(v)
    prev = lambda t: jnp.pad(t, ((0, 0), (0, 0), (0, 0), (1, 0), (0, 0), (0, 0)))[:, :, :, :-1]
    kb = jnp.concatenate([prev(ks), ks], axis=4)
    vb = jnp.concatenate([prev(vs), vs], axis=4)

    qi = jnp.arange(BLK)[:, None] + BLK
    kj = jnp.arange(2 * BLK)[None, :]
    dist = qi - kj
    band = (dist >= 0) & (dist <= span)
    blk = jnp.arange(nb)[:, None, None]
    valid = band[None] & ~((blk == 0) & (kj[None] < BLK))

    scale = 1.0 / math.sqrt(Dh)
    s = jnp.einsum('brhnqc,brhnkc->brhnqk', qs, kb,
                   preferred_element_type=jnp.float32) * scale
    s = jnp.where(valid, s, -1e30)
    m = jnp.max(s, axis=-1, keepdims=True)
    p = jnp.exp(s - m)
    l = jnp.sum(p, axis=-1, keepdims=True)
    o = jnp.einsum('brhnqk,brhnkc->brhnqc', p, vb.astype(jnp.float32)) / l
    lse = (m + jnp.log(l))[..., 0]

    o = o.reshape(Bn, dil, H, L, Dh).transpose(0, 3, 1, 2, 4).reshape(Bn, S_pad, H, Dh)[:, :S]
    lse = lse.reshape(Bn, dil, H, L).transpose(0, 3, 1, 2).reshape(Bn, S_pad, H)[:, :S]
    return o, lse

def dilated_attention_mixture(q, k, v):
    outs, lses = [], []
    for g, (window, dil) in enumerate(A_GROUPS):
        o, lse = dilated_window_attention(q[:, :, g], k[:, :, g], v[:, :, g], window, dil)
        outs.append(o)
        lses.append(lse)
    w = jax.nn.softmax(jnp.stack(lses, axis=0), axis=0)
    o = jnp.sum(w[..., None] * jnp.stack(outs, axis=0), axis=0)
    Bn, S = o.shape[:2]
    return o.reshape(Bn, S, A_OUT).astype(q.dtype)

def spatial_gating(u, v, w_s, b_s, ln_g, ln_b):
    v = layer_norm(v, ln_g, ln_b)
    Bn, S, _ = v.shape
    nc = S // B_CHUNK
    vc = v.reshape(Bn, nc, B_CHUNK, B_GROUPS, B_GROUP_DIM)
    causal = jnp.tril(jnp.ones((B_CHUNK, B_CHUNK), dtype=bool))
    w = jnp.where(causal[None], w_s, 0.0).astype(v.dtype)
    mixed = jnp.einsum('gts,bnsgc->bntgc', w, vc) + b_s.T[None, None, :, :, None]
    return u * mixed.reshape(Bn, S, B_WIDTH)

def multiscale_pool(xc, w_c, scale_c):
    Bn, S, _ = xc.shape
    xg = xc.reshape(Bn, S, C_GROUPS, C_GROUP_DIM).astype(jnp.float32)
    cs = jnp.cumsum(xg, axis=1)
    t1 = jnp.arange(1, S + 1, dtype=jnp.float32)
    pooled = []
    for gi, w in enumerate(C_WINDOWS):
        c = cs[:, :, gi]
        shifted = jnp.pad(c, ((0, 0), (w, 0), (0, 0)))[:, :S]
        cnt = jnp.minimum(t1, float(w))[None, :, None]
        pooled.append((c - shifted) / cnt - xg[:, :, gi])
    pooled = jnp.stack(pooled, axis=2)
    y = jnp.einsum('bsgc,gcd->bsgd', pooled, w_c.astype(jnp.float32)) * scale_c.astype(jnp.float32)
    return y.reshape(Bn, S, C_WIDTH).astype(xc.dtype)

def setup_inputs(seed: int = 0) -> dict:
    key = jax.random.key(seed)
    ks = jax.random.split(key, 32)
    f32 = jnp.float32
    nrm = lambda k, shape, fan_in: jax.random.normal(k, shape, f32) * (fan_in ** -0.5)
    gain = lambda k, shape: 1.0 + 0.05 * jax.random.normal(k, shape, f32)
    small = lambda k, shape: 0.01 * jax.random.normal(k, shape, f32)
    L = DEPTH
    return {
        "x": jax.random.normal(ks[0], (BATCH, SEQ, D_MODEL), f32),
        "ffn1_norm": gain(ks[1], (L, D_MODEL)),
        "ffn1_w_gate": nrm(ks[2], (L, D_MODEL, D_FF), D_MODEL),
        "ffn1_w_up": nrm(ks[3], (L, D_MODEL, D_FF), D_MODEL),
        "ffn1_w_down": nrm(ks[4], (L, D_FF, D_MODEL), D_FF),
        "mix_norm": gain(ks[5], (L, D_MODEL)),
        "w_in": nrm(ks[6], (L, D_MODEL, IN_WIDTH), D_MODEL),
        "b_gate": small(ks[7], (L, N_BRANCH * D_MODEL)),
        "b_ln_g": gain(ks[8], (L, B_WIDTH)),
        "b_ln_b": small(ks[9], (L, B_WIDTH)),
        "b_w_s": nrm(ks[10], (L, B_GROUPS, B_CHUNK, B_CHUNK), B_CHUNK),
        "b_b_s": gain(ks[11], (L, B_GROUPS, B_CHUNK)),
        "c_w": nrm(ks[12], (L, C_GROUPS, C_GROUP_DIM, C_GROUP_DIM), C_GROUP_DIM),
        "c_scale": gain(ks[13], (L, C_GROUPS, C_GROUP_DIM)),
        "w_proj_a": nrm(ks[14], (L, A_OUT, D_MODEL), A_OUT),
        "w_proj_b": nrm(ks[15], (L, B_WIDTH, D_MODEL), B_WIDTH),
        "w_proj_c": nrm(ks[16], (L, C_WIDTH, D_MODEL), C_WIDTH),
        "w_out": nrm(ks[17], (L, D_MODEL, D_MODEL), D_MODEL),
        "ffn2_norm": gain(ks[18], (L, D_MODEL)),
        "ffn2_w_gate": nrm(ks[19], (L, D_MODEL, D_FF), D_MODEL),
        "ffn2_w_up": nrm(ks[20], (L, D_MODEL, D_FF), D_MODEL),
        "ffn2_w_down": nrm(ks[21], (L, D_FF, D_MODEL), D_FF),
        "final_norm": gain(ks[22], (D_MODEL,)),
    }

def reference(x, ffn1_norm, ffn1_w_gate, ffn1_w_up, ffn1_w_down, mix_norm, w_in, b_gate,
              b_ln_g, b_ln_b, b_w_s, b_b_s, c_w, c_scale, w_proj_a, w_proj_b, w_proj_c,
              w_out, ffn2_norm, ffn2_w_gate, ffn2_w_up, ffn2_w_down, final_norm):
    Bn, S, D = x.shape
    for i in range(DEPTH):
        x = x + 0.5 * swiglu(rms_norm(x, ffn1_norm[i]), ffn1_w_gate[i], ffn1_w_up[i], ffn1_w_down[i])

        h = rms_norm(x, mix_norm[i])
        z = h @ w_in[i]
        qkv_shape = (Bn, S, A_N_GROUPS, A_HEADS_PER_GROUP, HEAD_DIM)
        q = z[..., Q_OFF:K_OFF].reshape(qkv_shape)
        k = z[..., K_OFF:V_OFF].reshape(qkv_shape)
        v = z[..., V_OFF:UB_OFF].reshape(qkv_shape)
        y_a = dilated_attention_mixture(q, k, v)

        uv = jax.nn.gelu(z[..., UB_OFF:C_OFF], approximate=False)
        y_b = spatial_gating(uv[..., :B_WIDTH], uv[..., B_WIDTH:], b_w_s[i], b_b_s[i],
                             b_ln_g[i], b_ln_b[i])

        y_c = multiscale_pool(z[..., C_OFF:G_OFF], c_w[i], c_scale[i])

        gates = jax.nn.sigmoid(z[..., G_OFF:] + b_gate[i]).reshape(Bn, S, N_BRANCH, D)
        merged = (gates[:, :, 0] * (y_a @ w_proj_a[i])
                  + gates[:, :, 1] * (y_b @ w_proj_b[i])
                  + gates[:, :, 2] * (y_c @ w_proj_c[i]))
        x = x + merged @ w_out[i]

        x = x + 0.5 * swiglu(rms_norm(x, ffn2_norm[i]), ffn2_w_gate[i], ffn2_w_up[i], ffn2_w_down[i])
    return rms_norm(x, final_norm)


_drawn_inputs = setup_inputs


def setup_inputs(seed=0):
    import zlib

    import numpy as np

    out = dict(_drawn_inputs(seed))
    spreads = {}
    factors = {'b_gate': 8.0,
     'b_ln_g': 4.196,
     'b_ln_b': 31.628,
     'b_b_s': 2.793,
     'c_scale': 2.969,
     'ffn2_norm': 3.483}
    for name, (base, spread) in spreads.items():
        noise = np.random.default_rng([zlib.crc32(name.encode()), seed]).standard_normal(out[name].shape)
        drawn = base * np.exp(spread * noise) if base else spread * noise
        out[name] = __import__('jax').numpy.asarray(drawn.astype(out[name].dtype))
    for name, factor in factors.items():
        out[name] = (out[name] * factor).astype(out[name].dtype)
    return out
```

```python
from contextlib import ExitStack, contextmanager

import concourse.bass as bass
from concourse import mybir

F32 = mybir.dt.float32
F32R = mybir.dt.float32r
BF16 = mybir.dt.bfloat16
I32 = mybir.dt.int32
ALU = mybir.AluOpType
ACT = mybir.ActivationFunctionType

P = 128
EPS = 1e-6
HEAD_DIM = 64
HEADS = 4
GROUPS = 3
WINDOW0 = 128
RES = 4
CHUNK = 128
POOL_WINDOWS = (2, 4, 8, 16)
PAD = 16
MASKED = -1e30
UNIT_K = 8
UNIT_N = 256


class Count:

    def __init__(self, start=0):
        self.base, self.local, self.outer = start, 0, []

    def next(self, n=1):
        self.local += n
        return self.base + self.local

    def now(self, more=0):
        return self.base + (self.local + more)

    def enter(self, i, per):
        self.outer.append((self.base, self.local))
        self.base, self.local = self.base + self.local + i * per, 0

    def leave(self, rounds, per):
        base, local = self.outer.pop()
        self.base, self.local = base, local + rounds * per


@contextmanager
def rounds(eng, n, counts, **per):
    with eng.Fori(0, n) as i:
        for name, c in counts.items():
            c.enter(i, per.get(name, 0))
        yield i
        wrong = {name: c.local for name, c in counts.items() if c.local != per.get(name, 0)}
        assert not wrong, wrong
    for name, c in counts.items():
        c.leave(n, per.get(name, 0))


def trunk(nc, x, ffn1_norm, ffn1_w_gate, ffn1_w_up, ffn1_w_down, mix_norm, w_in, b_gate, b_ln_g,
          b_ln_b, b_w_s, b_b_s, c_w, c_scale, w_proj_a, w_proj_b, w_proj_c, w_out, ffn2_norm,
          ffn2_w_gate, ffn2_w_up, ffn2_w_down, final_norm, out):
    DEPTH, D, FF = ffn1_w_gate.shape
    S = x.shape[1]
    KD = D // P
    KF = FF // P
    FF_UNITS = FF // UNIT_N
    D_PAIRS = D // UNIT_N
    TILES = S // P
    A_OUT = HEADS * HEAD_DIM
    A_WIDTH = GROUPS * A_OUT
    BW = b_ln_g.shape[1]
    KA, KB = A_OUT // P, BW // P
    V_N = A_WIDTH // 4
    Q_OFF, K_OFF, V_OFF = 0, A_WIDTH, 2 * A_WIDTH
    UB_OFF = 3 * A_WIDTH
    VB_OFF, C_OFF, G_OFF = UB_OFF + BW, UB_OFF + 2 * BW, UB_OFF + 3 * BW
    ATT = HEADS * RES
    KEYS = S + 2 * P
    DOWN_K = [(k, min(k + UNIT_K, KF)) for k in range(0, KF, UNIT_K)]
    assert (S, D, TILES, RES, KD) == (4 * P, 8 * P, 4, 4, 8) and len(DOWN_K) == 3
    assert FF % UNIT_N == 0 and D_PAIRS == 4 and BW == 2 * UNIT_N == S

    with ExitStack() as ctx:
        base = 16512
        def at(name, offset, cols, dt=F32):
            return nc.alloc_sbuf_tensor_at(name, [P, cols], dt, offset=base + offset)

        KB_ = 1024
        xT = at("xT", 0, KD * S)
        h_hi = at("h_hi", 16 * KB_, KD * S, F32R)
        h_lo = at("h_lo", 32 * KB_, KD * S, F32R)
        raw = [at(f"raw{s}", (48 + 8 * s) * KB_, UNIT_K * UNIT_N) for s in range(2)]
        w_hi = [at(f"w_hi{s}", (64 + 16 * s) * KB_, UNIT_K * UNIT_N, F32R) for s in range(2)]
        w_lo = [at(f"w_lo{s}", (72 + 16 * s) * KB_, UNIT_K * UNIT_N, F32R) for s in range(2)]
        rstd = at("rstd", 96 * KB_, S)
        acc = at("acc", 98 * KB_, 2 * S)
        gs = at("gs", 102 * KB_, 2 * S)
        us = at("us", 106 * KB_, 2 * S)
        masks = at("masks", 110 * KB_, RES * KEYS, BF16)
        ident = at("ident", 116 * KB_, P)
        ones = at("ones", 116 * KB_ + 512, P)
        table = at("table", 117 * KB_, P)
        small = at("small", 117 * KB_ + 512, P)
        M = 118 * KB_
        act_hi = at("act_hi", M, KF * S, F32R)
        act_lo = at("act_lo", M + KF * S * 4, KF * S, F32R)
        x_in = at("x_in", M, TILES * D)
        vectors = at("vectors", M + 16 * KB_, P)
        index_i = at("index_i", M + 17 * KB_, P, I32)
        index_f = at("index_f", M + 18 * KB_, P)
        mask_f = at("mask_f", M + 20 * KB_, RES * KEYS)
        x_out = at("x_out", M, TILES * D)
        gain_rows = at("gain_rows", M + 16 * KB_, D)
        vb = at("vb", M, TILES * BW)
        w_s = at("w_s", M + 8 * KB_, KB * CHUNK)
        bias_s = at("bias_s", M + 10 * KB_, KB * CHUNK)
        ln_g = at("ln_g", M + 12 * KB_, BW)
        ln_b = at("ln_b", M + 14 * KB_, BW)
        cw = at("cw", M + 16 * KB_, KB * P)
        w_sT = at("w_sT", M + 18 * KB_, KB * CHUNK)
        CP = PAD + S
        c_pad = at("c_pad", M + 24 * KB_, 4 * CP)
        sums = [at(f"sums{s}", M + 36 * KB_ + s * 3 * KB_, CP) for s in range(2)]
        qT = at("qT", M, 6 * S)
        kT = at("kT", M + 12 * KB_, 6 * S)
        v = at("v", M + 24 * KB_, TILES * A_WIDTH)
        p_tile = [at(f"p_tile{s}", M + 36 * KB_ + s * 3 * KB_, KEYS) for s in range(2)]
        pT = at("pT", M + 42 * KB_, KEYS)
        ya_hi = at("ya_hi", M + 45 * KB_, KA * S, F32R)
        ya_lo = at("ya_lo", M + 49 * KB_, KA * S, F32R)
        ub = at("ub", M + 53 * KB_, KB * S)
        yb_hi = at("yb_hi", M + 53 * KB_, KB * S, F32R)
        yb_lo = at("yb_lo", M + 61 * KB_, KB * S, F32R)
        yc_hi = at("yc_hi", M + 69 * KB_, KB * S, F32R)
        yc_lo = at("yc_lo", M + 77 * KB_, KB * S, F32R)
        m_hi = at("m_hi", M, KD * S, F32R)
        m_lo = at("m_lo", M + 16 * KB_, KD * S, F32R)
        gate = [at(f"gate{g}", M + (32 + 4 * g) * KB_, 2 * S) for g in range(3)]

        norm_cols = small[:, 0:8]
        ln_stats = small[:, 8:32]
        ln_mv = small[:, 32:40]
        ln_rs = small[:, 40:44]
        neg_max = small[:, 44:46]
        row_max = small[:, 46:48]
        row_sum = small[:, 48:50]
        row_inv = small[:, 50:52]
        inv_count = small[:, 64:64 + PAD]
        pool_head = small[:, 80:80 + PAD]
        T_FFN1, T_MIX, T_FFN2, T_FINAL = 0, DEPTH * KD, 2 * DEPTH * KD, 3 * DEPTH * KD
        T_BGATE = T_FINAL + KD
        T_CSCALE = T_BGATE + DEPTH * 3 * KD
        N_VEC = T_CSCALE + DEPTH * KB
        assert N_VEC <= P

        psum = [ctx.enter_context(nc.psum_tensor(f"psum{s}", [P, 2 * S], F32)) for s in range(2)]
        side = [ctx.enter_context(nc.psum_tensor(f"side{s}", [P, 2 * S], F32)) for s in range(2)]

        def sem(name):
            return ctx.enter_context(nc.semaphore(name))

        x_loaded = sem("x_loaded")
        vectors_loaded = sem("vectors_loaded")
        params_loaded = sem("params_loaded")
        gains_loaded = sem("gains_loaded")
        stored = sem("stored")
        consts_made = sem("consts_made")
        mask_step = sem("mask_step")
        table_made = sem("table_made")
        raw_loaded = [sem(f"raw_loaded{s}") for s in range(2)]
        hi_made = sem("hi_made")
        split_made = sem("split_made")
        unit_done = sem("unit_done")
        evacuated = [sem(f"evacuated{s}") for s in range(2)]
        side_done = [sem(f"side_done{s}") for s in range(2)]
        side_evacuated = [sem(f"side_evacuated{s}") for s in range(2)]
        h_hi_made = sem("h_hi_made")
        sq_made = sem("sq_made")
        h_ready = sem("h_ready")
        acc_ready = sem("acc_ready")
        std_made = sem("std_made")
        rstd_made = sem("rstd_made")
        silu_made = sem("silu_made")
        act_made = sem("act_made")
        act_hi_made = sem("act_hi_made")
        act_ready = sem("act_ready")
        w_sT_made = sem("w_sT_made")
        pooled = sem("pooled")
        yc_hi_made = sem("yc_hi_made")
        gelu_made = sem("gelu_made")
        ln_var_made = sem("ln_var_made")
        ln_std_made = sem("ln_std_made")
        vb_ready = sem("vb_ready")
        yb_made = sem("yb_made")
        yb_hi_made = sem("yb_hi_made")
        neg_max_made = sem("neg_max_made")
        exp_made = sem("exp_made")
        p_made = sem("p_made")
        pT_written = sem("pT_written")
        head_done = sem("head_done")
        ya_hi_made = sem("ya_hi_made")
        head_made = sem("head_made")
        y_ready = sem("y_ready")
        gate_made = sem("gate_made")
        merged_made = sem("merged_made")
        merged_hi_made = sem("merged_hi_made")
        merged_ready = sem("merged_ready")
        dve_step = sem("dve_step")
        turned = sem("turned")
        out_made = sem("out_made")

        PER_DOWN_HALF = dict(unit_done=6, ev0=1, ev1=1)
        down_counts = PER_DOWN_HALF

        block = ctx.enter_context(nc.Block())

        def pair(t, d, n=2 * S):
            return t[:, bass.ds(d * (2 * S), n)]

        @block.sync
        def _(sp):
            row = 0
            for vec in (ffn1_norm, mix_norm, ffn2_norm):
                for l in range(DEPTH):
                    sp.dma_start(vectors[row:row + KD, :], vec[l].rearrange("(k p) -> k p", p=P)) \
                      .then_inc(vectors_loaded, 16)
                    row += KD
            sp.dma_start(vectors[row:row + KD, :], final_norm.rearrange("(k p) -> k p", p=P)) \
              .then_inc(vectors_loaded, 16)
            row += KD
            for l in range(DEPTH):
                sp.dma_start(vectors[row:row + 3 * KD, :], b_gate[l].rearrange("(k p) -> k p", p=P)) \
                  .then_inc(vectors_loaded, 16)
                row += 3 * KD
            for l in range(DEPTH):
                sp.dma_start(vectors[row:row + KB, :], c_scale[l]).then_inc(vectors_loaded, 16)
                row += KB

            counts = dict(split_made=Count(), slot=Count())

            def load(parts):
                slot = load.slot
                sp.wait_ge(split_made, counts["split_made"].next())
                n = parts[0][0].shape[2]
                dst = raw[slot][:, 0:UNIT_K * n].rearrange("p (k n) -> p k n", n=n)
                for src, k in parts:
                    sp.dma_start(dst[:, k:k + src.shape[1], :], src).then_inc(raw_loaded[slot], 16)
                load.slot = 1 - slot
            load.slot = 0

            def view(w, layer, col, n, k0=0, k1=None):
                src = w[bass.ds(layer, 1)].rearrange("a (k p) n -> p (a k) n", p=P)
                return src[:, k0:k1 or src.shape[1], bass.ds(col, n)]

            def load_ffn(layer, w_gate, w_up, w_down):
                with rounds(sp, FF_UNITS, counts, split_made=2) as i:
                    for w in (w_gate, w_up):
                        load([(view(w, layer, i * UNIT_N, UNIT_N), 0)])
                with rounds(sp, D_PAIRS // 2, counts, split_made=2 * len(DOWN_K)) as half:
                    for d in range(2):
                        for k0, k1 in DOWN_K:
                            load([(view(w_down, layer, half * (2 * UNIT_N) + d * UNIT_N, UNIT_N, k0, k1), 0)])

            UNITS = 4 * FF_UNITS + 4 * len(DOWN_K) * 2 + 16 + 5 * D_PAIRS + D_PAIRS
            with rounds(sp, DEPTH, counts, split_made=UNITS) as layer:
                load_ffn(layer, ffn1_w_gate, ffn1_w_up, ffn1_w_down)
                for off in (C_OFF, UB_OFF, VB_OFF):
                    for u in range(2):
                        load([(view(w_in, layer, off + u * UNIT_N, UNIT_N), 0)])
                for u in range(4):
                    load([(view(w_in, layer, V_OFF + u * V_N, V_N), 0)])
                for off in (Q_OFF, K_OFF):
                    for u in range(GROUPS):
                        if off + u == 0:
                            load([(view(w_in, layer, 0, UNIT_N, UNIT_K // 2, UNIT_K), UNIT_K // 2),
                                  (view(w_in, layer, 0, UNIT_N, 0, UNIT_K // 2), 0)])
                        else:
                            load([(view(w_in, layer, off + u * UNIT_N, UNIT_N), 0)])
                with rounds(sp, D_PAIRS // 2, counts, split_made=10) as half:
                    for d in range(2):
                        col = half * (2 * UNIT_N) + d * UNIT_N
                        for g in range(3):
                            load([(view(w_in, layer, G_OFF + g * D + col, UNIT_N), 0)])
                        load([(view(w_proj_a, layer, col, UNIT_N), 0), (view(w_proj_b, layer, col, UNIT_N), KA)])
                        load([(view(w_proj_c, layer, col, UNIT_N), 0)])
                with rounds(sp, D_PAIRS // 2, counts, split_made=2) as half:
                    for d in range(2):
                        load([(view(w_out, layer, half * (2 * UNIT_N) + d * UNIT_N, UNIT_N), 0)])
                load_ffn(layer, ffn2_w_gate, ffn2_w_up, ffn2_w_down)

            sp.wait_ge(unit_done, DEPTH * UNITS + 2)
            sp.dma_start(gain_rows[:, :], final_norm.partition_broadcast(P)).then_inc(gains_loaded, 16)
            for b in range(TILES):
                sp.wait_ge(out_made, b + 1)
                sp.dma_start(out[0, b * P:(b + 1) * P, :], x_out[:, b * D:(b + 1) * D]).then_inc(stored, 16)
            sp.wait_ge(stored, 16 * TILES)

        UNITS_PER_LAYER = 4 * FF_UNITS + 4 * len(DOWN_K) * 2 + 16 + 5 * D_PAIRS + D_PAIRS

        @block.gpsimd
        def _(pool):
            def fill(t, c):
                nc.gpsimd.memset(t, c).then_inc(consts_made, 1)
            fill(ident[:, :], 0.0)
            fill(ones[:, :], 1.0)
            fill(mask_f[:, :], 0.0)
            pool.wait_ge(consts_made, 3)
            nc.gpsimd.affine_select(out=ident[:, :], in_=ident[:, :], compare_op=ALU.not_equal, fill=1.0,
                                    base=0, pattern=[[-1, P]], channel_multiplier=1).then_inc(consts_made, 1)
            nc.gpsimd.iota(index_i[:, :], pattern=[[-1, P]], base=S, channel_multiplier=1).then_inc(mask_step, 1)
            n = 1
            for r in range(RES):
                m0 = mask_f[:, r * KEYS:r * KEYS + S]
                for sign, base_ in ((1, r), (-1, WINDOW0 - r)):
                    nc.gpsimd.affine_select(out=m0, in_=m0, compare_op=ALU.is_ge, fill=MASKED, base=base_,
                                            pattern=[[-sign, RES], [-RES * sign, P]],
                                            channel_multiplier=RES * sign).then_inc(mask_step, 1)
                    n += 1
                    pool.wait_ge(mask_step, n)
                m12 = mask_f[:, r * KEYS + S:(r + 1) * KEYS]
                nc.gpsimd.affine_select(out=m12, in_=m12, compare_op=ALU.is_ge, fill=MASKED, base=0,
                                        pattern=[[0, 2], [-1, P]], channel_multiplier=1).then_inc(mask_step, 1)
                n += 1
            pool.wait_ge(mask_step, n)
            for layer in range(DEPTH):
                pool.wait_ge(side_evacuated[1], 3 + layer * 3)
                nc.gpsimd.affine_select(out=w_sT[:, :], in_=w_sT[:, :], compare_op=ALU.is_ge, fill=0.0, base=0,
                                        pattern=[[0, KB], [1, CHUNK]], channel_multiplier=-1).then_inc(w_sT_made, 1)
        MASK_STEPS = 1 + 3 * RES

        @block.tensor
        def _(pe):
            counts = {k: Count() for k in ("ev0", "ev1", "sv0", "sv1", "h", "acc", "act", "w_sT", "pooled",
                                           "vb", "p", "head", "y", "merged", "exp")}
            counts["unit"] = Count(2)
            pe_slot = [0]

            def begin(s):
                pe.wait_ge(evacuated[s], counts[f"ev{s}"].next())
                return psum[s]

            def begin_side(s):
                pe.wait_ge(side_evacuated[s], counts[f"sv{s}"].next())
                return side[s]

            def unit():
                pe.wait_ge(split_made, counts["unit"].next())
                slot = pe_slot[0]
                pe_slot[0] = 1 - slot
                return w_hi[slot], w_lo[slot]

            def columns(dst, w, x_hi, x_lo, ks, first, last, x_k0=0, need=None):
                whi, wlo = w
                for c in range(2):
                    o = dst[:, c * S:(c + 1) * S]
                    for k in ks:
                        if c == 0 and need:
                            need(k)
                        a = slice(k * UNIT_N + c * P, k * UNIT_N + (c + 1) * P)
                        b = slice((x_k0 + k) * S, (x_k0 + k + 1) * S)
                        for n, (l, r) in enumerate(((whi, x_hi), (whi, x_lo), (wlo, x_hi))):
                            mm = nc.tensor.matmul(o, l[:, a], r[:, b], start=first and k == ks[0] and n == 0,
                                                  stop=last and k == ks[-1] and n == 2)
                return mm

            def columns_open(dst, w, x_hi, x_lo, ks, first, last, x_k0):
                return columns(dst, w, x_hi, x_lo, ks, first, last, x_k0)

            def need_h(k):
                if k % 2 == 0:
                    pe.wait_ge(h_ready, counts["h"].next())

            def norm_sums(by_token):
                pe.wait_ge(acc_ready, counts["acc"].next(1 + D_PAIRS))
                o = begin_side(0)
                for c in range(2):
                    mm = nc.tensor.matmul(o[:, 0:S], ones[:, :], acc[:, c * S:(c + 1) * S], start=(c == 0), stop=(c == 1))
                if by_token:
                    mm = token_sums(o, S)
                mm.then_inc(side_done[0], 1)

            def token_sums(o, at_col):
                for t in range(2 * TILES):
                    for c in range(2):
                        a = acc[:, c * S:(c + 1) * S]
                        a = a[:, t * P:(t + 1) * P] if t < TILES else \
                            a.rearrange("p (i r) -> p r i", r=RES)[:, t - TILES, :]
                        mm = nc.tensor.matmul(o[:, at_col + t:at_col + t + 1], a, ones[:, 0:1], start=(c == 0), stop=(c == 1))
                return mm

            def ffn():
                o = begin(0)
                columns(o, unit(), h_hi, h_lo, range(KD), True, True, need=need_h).then_inc(unit_done, 1)
                norm_sums(False)
                o = begin(1)
                columns(o, unit(), h_hi, h_lo, range(KD), True, True).then_inc(unit_done, 1)
                with rounds(pe, FF_UNITS - 1, counts, unit=2, ev0=1, ev1=1) as i:
                    for s in range(2):
                        o = begin(s)
                        columns(o, unit(), h_hi, h_lo, range(KD), True, True).then_inc(unit_done, 1)
                counts["act"].next(FF_UNITS)
                with rounds(pe, D_PAIRS // 2, counts, unit=2 * len(DOWN_K), ev0=1, ev1=1) as half:
                    pe.wait_ge(act_ready, counts["act"].now())
                    for s in range(2):
                        o = begin(s)
                        for n, (k0, k1) in enumerate(DOWN_K):
                            columns(o, unit(), act_hi, act_lo, range(k1 - k0), n == 0, n == len(DOWN_K) - 1,
                                    x_k0=k0).then_inc(unit_done, 1)

            pe.wait_ge(consts_made, 4)
            pe.wait_ge(vectors_loaded, 16 * (3 * DEPTH + 1 + 2 * DEPTH))
            o = begin_side(1)
            nc.tensor.transpose(o[:, 0:N_VEC], vectors[0:N_VEC, :], ident[0:N_VEC, 0:N_VEC]).then_inc(side_done[1], 1)
            pe.wait_ge(x_loaded, 16 * TILES)
            for d in range(D_PAIRS):
                o = begin(d % 2)
                for c in range(2):
                    for t in range(TILES):
                        mm = nc.tensor.transpose(o[:, c * S + t * P:c * S + (t + 1) * P],
                                                 x_in[:, t * D + (2 * d + c) * P:t * D + (2 * d + c + 1) * P], ident[:, :])
                mm.then_inc(turned, 1)

            with rounds(pe, DEPTH, counts, unit=UNITS_PER_LAYER, ev0=48 + ATT // 2, ev1=48 + ATT // 2,
                        sv0=3 + 2 + ATT, sv1=3, h=3 * D_PAIRS, acc=3 * (1 + D_PAIRS), act=2 * FF_UNITS, w_sT=1, pooled=4,
                        vb=1, p=ATT, head=ATT, y=2, merged=D_PAIRS, exp=0) as layer:
                ffn()

                o = begin(0)
                columns(o, unit(), h_hi, h_lo, range(KD), True, True, need=need_h).then_inc(unit_done, 1)
                norm_sums(True)
                pe.wait_ge(head_made, counts["head"].now(2))
                pe.wait_ge(params_loaded, 16 * 5 + layer * (16 * 5))
                o = begin_side(1)
                for g in range(KB):
                    mm = nc.tensor.transpose(o[:, g * P:(g + 1) * P], w_s[:, g * P:(g + 1) * P], ident[:, :])
                mm.then_inc(side_done[1], 1)
                o = begin(1)
                columns(o, unit(), h_hi, h_lo, range(KD), True, True).then_inc(unit_done, 1)

                def pool_out(s):
                    pe.wait_ge(pooled, counts["pooled"].next(2))
                    o = begin_side(s)
                    for c in range(2):
                        g = 2 * s + c
                        mm = nc.tensor.matmul(o[:, c * S:(c + 1) * S], cw[:, g * P:(g + 1) * P],
                                              c_pad[:, g * CP + PAD:(g + 1) * CP], start=True, stop=True)
                    mm.then_inc(side_done[s], 1)

                for u in range(2):
                    o = begin(u)
                    columns(o, unit(), h_hi, h_lo, range(KD), True, True).then_inc(unit_done, 1)
                    pool_out(u)

                def rows(s, n, x_of):
                    o = begin(s)
                    whi, wlo = unit()
                    for t in range(TILES):
                        d = o[:, t * UNIT_N:t * UNIT_N + n]
                        for k in range(KD):
                            b = slice(k * n, (k + 1) * n)
                            for m, (l, r) in enumerate(((h_hi, whi), (h_lo, whi), (h_hi, wlo))):
                                mm = nc.tensor.matmul(d, x_of(l[:, k * S:(k + 1) * S], t), r[:, b],
                                                      start=(k == 0 and m == 0), stop=(k == KD - 1 and m == 2))
                    mm.then_inc(unit_done, 1)

                natural = lambda a, t: a[:, t * P:(t + 1) * P]
                residue = lambda a, t: a.rearrange("p (i r) -> p r i", r=RES)[:, t, :]
                for u in range(2):
                    rows(u, UNIT_N, natural)
                for u in range(4):
                    rows(u % 2, V_N, residue)
                    if u in (1, 2):
                        s = u - 1
                        if u == 1:
                            pe.wait_ge(w_sT_made, counts["w_sT"].next())
                            pe.wait_ge(vb_ready, counts["vb"].next())
                        o = begin_side(s)
                        for c in range(2):
                            g = 2 * s + c
                            for t in range(TILES):
                                mm = nc.tensor.matmul(o[:, c * S + t * P:c * S + (t + 1) * P],
                                                      vb[:, t * BW + g * P:t * BW + (g + 1) * P],
                                                      w_sT[:, g * P:(g + 1) * P], start=True, stop=True)
                        mm.then_inc(side_done[s], 1)
                for u in range(2 * GROUPS):
                    o = begin(u % 2)
                    columns(o, unit(), h_hi, h_lo, range(KD), True, True).then_inc(unit_done, 1)

                pe.wait_ge(evacuated[0], counts["ev0"].now(1))
                pe.wait_ge(evacuated[1], counts["ev1"].now(1))
                pe.wait_ge(side_evacuated[1], counts["sv1"].now(1))

                def scores(n):
                    j, r = divmod(n, RES)
                    rows_ = slice((j % 2) * HEAD_DIM, (j % 2 + 1) * HEAD_DIM)
                    o = begin_side(0)
                    col = 0
                    for g in range(GROUPS):
                        c = (2 * g + j // 2) * S
                        keys = kT[rows_, c:c + S] if g == 0 else kT[rows_, c + r * P:c + (r + 1) * P]
                        width = S if g == 0 else P
                        mm = nc.tensor.matmul(o[:, col:col + width], qT[rows_, c + r * P:c + (r + 1) * P], keys,
                                              start=True, stop=True)
                        col += width
                    mm.then_inc(side_done[0], 1)

                scores(0)
                for n in range(ATT):
                    j, r = divmod(n, RES)
                    if n + 1 < ATT:
                        scores(n + 1)
                    pe.wait_ge(p_made, counts["p"].next())
                    o = begin(n % 2)
                    for c in range(KEYS // P):
                        mm = nc.tensor.transpose(o[:, c * P:(c + 1) * P], p_tile[n % 2][:, c * P:(c + 1) * P], ident[:, :])
                    mm.then_inc(pT_written, 1)
                    pe.wait_ge(evacuated[n % 2], counts[f"ev{n % 2}"].now(1))
                    pe.wait_ge(head_made, counts["head"].next())
                    out_rows = slice((j % 2) * HEAD_DIM, (j % 2 + 1) * HEAD_DIM)
                    o = side[1][out_rows, (n % 2) * S:(n % 2) * S + P]
                    for c in range(KEYS // P):
                        g, t = (0, c) if c < TILES else (c - TILES + 1, r)
                        col = t * A_WIDTH + g * A_OUT + j * HEAD_DIM
                        mm = nc.tensor.matmul(o, v[:, col:col + HEAD_DIM], pT[:, c * P:(c + 1) * P],
                                              start=(c == 0), stop=(c == KEYS // P - 1))
                    mm.then_inc(head_done, 1)

                counts["y"].next(2)
                with rounds(pe, D_PAIRS // 2, counts, unit=10, ev0=6, ev1=6) as half:
                    pe.wait_ge(head_made, counts["head"].now(2))
                    pe.wait_ge(y_ready, counts["y"].now())
                    for d in range(2):
                        for g in range(3):
                            o = begin(g % 2)
                            columns(o, unit(), h_hi, h_lo, range(KD), True, True).then_inc(unit_done, 1)
                        w = unit()
                        columns(begin(1), w, ya_hi, ya_lo, range(KA), True, True)
                        columns(begin(0), w, yb_hi, yb_lo, range(KA, KA + KB), True, True, x_k0=-KA).then_inc(unit_done, 1)
                        columns(begin(1), unit(), yc_hi, yc_lo, range(KB), True, True).then_inc(unit_done, 1)
                counts["merged"].next(D_PAIRS)
                with rounds(pe, D_PAIRS // 2, counts, unit=2, ev0=1, ev1=1) as half:
                    pe.wait_ge(merged_ready, counts["merged"].now())
                    for s in range(2):
                        columns(begin(s), unit(), m_hi, m_lo, range(KD), True, True).then_inc(unit_done, 1)
                ffn()

            pe.wait_ge(acc_ready, counts["acc"].next(1 + D_PAIRS))
            o = begin_side(0)
            token_sums(o, 0).then_inc(side_done[0], 1)
            for t in range(TILES):
                o = begin(t % 2) if t < 2 else psum[t % 2]
                if t >= 2:
                    pe.wait_ge(out_made, t - 1)
                for k in range(KD):
                    mm = nc.tensor.transpose(o[:, k * P:(k + 1) * P], xT[:, k * S + t * P:k * S + (t + 1) * P], ident[:, :])
                mm.then_inc(turned, 1)

        @block.scalar
        def _(act):
            counts = {k: Count(1) for k in ("ev0", "ev1", "se0")}
            counts |= {k: Count() for k in ("unit", "raw0", "raw1", "act", "sd0", "sd1", "ln", "yb", "neg",
                                            "pT_written", "head", "merged")}
            slot = [0]

            def split():
                s = slot[0]
                slot[0] = 1 - s
                k, n, parts = split.shapes.pop(0) if split.shapes else (UNIT_K, UNIT_N, 1)
                act.wait_ge(raw_loaded[s], counts[f"raw{s}"].next(16 * parts))
                act.wait_ge(unit_done, counts["unit"].now(2))
                nc.scalar.activation(w_hi[s][:, 0:k * n], raw[s][:, 0:k * n], ACT.Copy).then_inc(hi_made, 1)
            split.shapes = []

            def residual(layer, gain, d, s):
                act.wait_ge(evacuated[s], counts[f"ev{s}"].next())
                for c in range(2):
                    a = bass.ds(d * (2 * S) + c * S, S)
                    mm = nc.scalar.activation(h_hi[:, a], xT[:, a], ACT.Copy,
                                              scale=table[:, bass.ds(gain + 2 * d + c, 1)])
                mm.then_inc(h_hi_made, 1)
                nc.scalar.activation(us[:, :], pair(xT, d), ACT.Square).then_inc(sq_made, 1)

            def root(cols=None):
                counts["sd0"].next()
                act.wait_ge(side_evacuated[0], counts["se0"].next())
                if cols is not None:
                    nc.scalar.activation(cols, cols, ACT.Sqrt)
                nc.scalar.activation(rstd[:, :], rstd[:, :], ACT.Sqrt).then_inc(std_made, 1)

            def step(ahead=True):
                if ahead:
                    split()
                counts["unit"].next()

            DOWN_SHAPES = [(k1 - k0, UNIT_N, 1) for k0, k1 in DOWN_K]

            def ffn(layer, gain, last):
                def inner(first, shape=None):
                    split()
                    counts["unit"].next()
                    if first:
                        root()
                    act.wait_ge(evacuated[0], counts["ev0"].next())
                    nc.scalar.activation(gs[:, :], gs[:, :], ACT.Silu).then_inc(silu_made, 1)
                    if shape:
                        split.shapes = [shape]
                    split()
                    counts["unit"].next()
                    counts["ev1"].next()
                def inner_hi(i):
                    act.wait_ge(act_made, counts["act"].next())
                    nc.scalar.activation(pair(act_hi, i), us[:, :], ACT.Copy).then_inc(act_hi_made, 1)
                inner(True)
                inner_hi(0)
                with rounds(act, FF_UNITS - 2, counts, unit=2, raw0=16, raw1=16, ev0=1, ev1=1, act=1) as i:
                    inner(False)
                    inner_hi(i + 1)
                inner(False, DOWN_SHAPES[0])
                inner_hi(FF_UNITS - 1)
                for d in range(D_PAIRS):
                    for n in range(3):
                        end = d == D_PAIRS - 1 and n == 2
                        if not (end and last):
                            split.shapes = [DOWN_SHAPES[(n + 1) % 3] if not end else (UNIT_K, UNIT_N, 1)]
                            split()
                        counts["unit"].next()
                    residual(layer, gain, d, d % 2)

            act.dma_start(x_in[:, 0:D], x[0, 0:P, :]).then_inc(x_loaded, 16)
            for t in range(1, TILES):
                act.dma_start(x_in[:, t * D:(t + 1) * D], x[0, t * P:(t + 1) * P, :]).then_inc(x_loaded, 16)
            act.wait_ge(side_done[1], counts["sd1"].next())
            nc.scalar.activation(table[:, 0:N_VEC], side[1][:, 0:N_VEC], ACT.Copy).then_inc(side_evacuated[1], 1)
            act.wait_ge(side_evacuated[1], 2)
            for d in range(D_PAIRS):
                residual(0, T_FFN1, d, d % 2)

            with rounds(act, DEPTH, counts, unit=UNITS_PER_LAYER, raw0=8 * (UNITS_PER_LAYER + D_PAIRS) + 16,
                        raw1=8 * (UNITS_PER_LAYER + D_PAIRS), ev0=48 + ATT // 2, ev1=48 + ATT // 2, se0=5 + ATT, act=2 * FF_UNITS,
                        sd0=5 + ATT, sd1=3, ln=1, yb=2, neg=ATT, pT_written=ATT, head=ATT, merged=D_PAIRS) as layer:
                split()
                ffn(layer, layer * KD + T_MIX, False)

                act.dma_start(w_s[:, :].rearrange("p (g s) -> p g s", s=CHUNK),
                              b_w_s[bass.ds(layer, 1)].rearrange("a g t s -> t (a g) s")).then_inc(params_loaded, 16)
                act.dma_start(cw[:, :].rearrange("p (g s) -> p g s", s=P),
                              c_w[bass.ds(layer, 1)].rearrange("a g t s -> t (a g) s")).then_inc(params_loaded, 16)
                act.dma_start(bias_s[:, :], b_b_s[bass.ds(layer, 1)].rearrange("a g s -> (a g s)").partition_broadcast(P)).then_inc(params_loaded, 16)
                act.dma_start(ln_g[:, :], b_ln_g[bass.ds(layer, 1)].rearrange("a s -> (a s)").partition_broadcast(P)).then_inc(params_loaded, 16)
                act.dma_start(ln_b[:, :], b_ln_b[bass.ds(layer, 1)].rearrange("a s -> (a s)").partition_broadcast(P)).then_inc(params_loaded, 16)

                step()
                root(norm_cols)
                counts["ev0"].next()
                act.wait_ge(side_done[1], counts["sd1"].next())
                nc.scalar.activation(w_sT[:, :], side[1][:, 0:KB * P], ACT.Copy).then_inc(side_evacuated[1], 1)
                step()
                counts["ev1"].next()

                def pool_hi(s):
                    act.wait_ge(side_done[s], counts[f"sd{s}"].next())
                    if s == 0:
                        counts["se0"].next()
                    for c in range(2):
                        g = 2 * s + c
                        mm = nc.scalar.activation(yc_hi[:, g * S:(g + 1) * S], side[s][:, c * S:(c + 1) * S], ACT.Copy,
                                                  scale=table[:, bass.ds(T_CSCALE + layer * KB + g, 1)])
                    mm.then_inc(yc_hi_made, 1)

                for u in range(2):
                    step()
                    act.wait_ge(evacuated[u], counts[f"ev{u}"].next())
                    nc.scalar.activation(pair(ub, u), pair(ub, u), ACT.Gelu).then_inc(gelu_made, 1)
                    pool_hi(u)
                act.wait_ge(rstd_made, 2 + layer * 3)
                for u in range(2):
                    if u == 1:
                        split.shapes = [(UNIT_K, V_N, 1)]
                    step()
                    act.wait_ge(unit_done, counts["unit"].now(2))
                    for t in range(TILES):
                        mm = nc.scalar.activation(vb[:, t * BW + u * UNIT_N:t * BW + (u + 1) * UNIT_N],
                                                  psum[u][:, t * UNIT_N:(t + 1) * UNIT_N], ACT.Gelu,
                                                  scale=norm_cols[:, t:t + 1])
                    mm.then_inc(evacuated[u], 1)
                    counts[f"ev{u}"].next()
                act.wait_ge(ln_var_made, counts["ln"].next())
                nc.scalar.activation(ln_rs, ln_rs, ACT.Sqrt).then_inc(ln_std_made, 1)
                for u in range(4):
                    split.shapes = [(UNIT_K, V_N, 1) if u < 3 else (UNIT_K, UNIT_N, 2)]
                    step()
                    act.wait_ge(unit_done, counts["unit"].now(2))
                    for t in range(TILES):
                        mm = nc.scalar.activation(v[:, t * A_WIDTH + u * V_N:t * A_WIDTH + (u + 1) * V_N],
                                                  psum[u % 2][:, t * UNIT_N:t * UNIT_N + V_N], ACT.Copy,
                                                  scale=norm_cols[:, TILES + t:TILES + t + 1])
                    mm.then_inc(evacuated[u % 2], 1)
                    counts[f"ev{u % 2}"].next()
                    if u in (2, 3):
                        act.wait_ge(yb_made, counts["yb"].next())
                        nc.scalar.activation(pair(yb_hi, u - 2), gs[:, :], ACT.Copy).then_inc(yb_hi_made, 1)
                for u in range(2 * GROUPS):
                    step()
                    counts[f"ev{u % 2}"].next()
                counts["sd0"].next(1 + ATT)
                counts["se0"].next(1 + ATT)
                counts["sd1"].next()

                def head_hi(n):
                    j, r = divmod(n, RES)
                    rows_ = slice((j % 2) * HEAD_DIM, (j % 2 + 1) * HEAD_DIM)
                    act.wait_ge(head_done, counts["head"].next())
                    dst = ya_hi[rows_, (j // 2) * S:(j // 2 + 1) * S].rearrange("p (i r) -> p r i", r=RES)[:, r, :]
                    nc.scalar.activation(dst, side[1][rows_, (n % 2) * S:(n % 2) * S + P],
                                         ACT.Copy).then_inc(ya_hi_made, 1)

                for n in range(ATT):
                    act.wait_ge(neg_max_made, counts["neg"].next())
                    nc.scalar.activation(p_tile[n % 2][:, :], p_tile[n % 2][:, :], ACT.Exp, bias=neg_max[:, n % 2:n % 2 + 1],
                                         accum_out=row_sum[:, n % 2:n % 2 + 1]).then_inc(exp_made, 1)
                    if n > 0:
                        head_hi(n - 1)
                    act.wait_ge(pT_written, counts["pT_written"].next())
                    nc.scalar.activation(pT[:, :], psum[n % 2][:, 0:KEYS], ACT.Copy).then_inc(evacuated[n % 2], 1)
                    counts[f"ev{n % 2}"].next()
                head_hi(ATT - 1)

                with rounds(act, D_PAIRS // 2, counts, unit=10, raw0=16 * 6, raw1=16 * 6, ev0=6, ev1=6, merged=2) as half:
                    for d in range(2):
                        for g in range(3):
                            if g == 2:
                                split.shapes = [(KA + KB, UNIT_N, 2)]
                            step()
                            act.wait_ge(evacuated[g % 2], counts[f"ev{g % 2}"].next())
                            for c in range(2):
                                mm = nc.scalar.activation(
                                    gate[g][:, c * S:(c + 1) * S], gate[g][:, c * S:(c + 1) * S], ACT.Sigmoid,
                                    bias=table[:, bass.ds(T_BGATE + layer * (3 * KD) + half * 4 + (g * KD + 2 * d + c), 1)])
                            mm.then_inc(gate_made, 1)
                        split.shapes = [(KB, UNIT_N, 1)]
                        step()
                        step()
                        counts["ev0"].next()
                        counts["ev1"].next(2)
                        act.wait_ge(merged_made, counts["merged"].next())
                        nc.scalar.activation(pair(m_hi, half * 2 + d), gate[0][:, :], ACT.Copy).then_inc(merged_hi_made, 1)
                with rounds(act, D_PAIRS // 2, counts, unit=2, raw0=16, raw1=16, ev0=1, ev1=1) as half:
                    for d in range(2):
                        step()
                        residual(layer, layer * KD + T_FFN2, half * 2 + d, d)
                ffn(layer, layer * KD + (T_FFN1 + KD), True)

            act.wait_ge(side_evacuated[0], counts["se0"].next())
            nc.scalar.activation(norm_cols, norm_cols, ACT.Sqrt).then_inc(std_made, 1)

        @block.vector
        def _(dve):
            counts = {k: Count() for k in ("unit", "hi", "step", "h_hi", "sq", "acc", "side0", "side1", "std", "rstd",
                                           "silu", "act_hi", "gelu", "ln_std", "yc_hi", "yb_hi", "exp",
                                           "head", "gate", "merged", "pooled", "y")}
            counts |= {k: Count(1) for k in ("ev0", "ev1", "se0", "se1")}
            slot = [0]

            def side_out(s, ins):
                ins.then_inc(side_evacuated[s], 1)
                return counts[f"se{s}"].next()

            def chain(ins):
                ins.then_inc(dve_step, 1)
                dve.wait_ge(dve_step, counts["step"].next())

            def split(k=UNIT_K, n=UNIT_N):
                s = slot[0]
                slot[0] = 1 - s
                dve.wait_ge(hi_made, counts["hi"].next())
                a = slice(0, k * n)
                nc.vector.tensor_tensor(w_lo[s][:, a], raw[s][:, a], w_hi[s][:, a].bitcast(F32),
                                        ALU.subtract).then_inc(split_made, 1)

            def step(k=UNIT_K, n=UNIT_N):
                split(k, n)
                done()

            def done():
                dve.wait_ge(unit_done, counts["unit"].next() + 2)

            def evac(s, ins):
                ins.then_inc(evacuated[s], 1)
                return counts[f"ev{s}"].next()

            rstd2 = rstd[:, :].unsqueeze(1).broadcast_to([P, 2, S])

            def two(t):
                return t.rearrange("p (c s) -> p c s", s=S)

            def scaled(dst, s):
                return nc.vector.tensor_tensor(dst, two(psum[s][:, :]), rstd2, ALU.mult)

            def residual(scale, gain, d, s):
                x_ = pair(xT, d)
                if scale is None:
                    v_ = evac(s, nc.vector.tensor_copy(x_, psum[s][:, :]))
                else:
                    v_ = evac(s, nc.vector.scalar_tensor_tensor(x_, psum[s][:, :], scale, x_, ALU.mult, ALU.add))
                dve.wait_ge(evacuated[s], v_)
                dve.wait_ge(h_hi_made, counts["h_hi"].next())
                for c in range(2):
                    a = bass.ds(d * (2 * S) + c * S, S)
                    i_ = nc.vector.scalar_tensor_tensor(h_lo[:, a], xT[:, a], table[:, bass.ds(gain + 2 * d + c, 1)],
                                                        h_hi[:, a].bitcast(F32), ALU.mult, ALU.subtract)
                i_.then_inc(h_ready, 1)
                dve.wait_ge(sq_made, counts["sq"].next())
                dve.wait_ge(acc_ready, counts["acc"].now())
                nc.vector.tensor_tensor(acc[:, :], acc[:, :], us[:, :], ALU.add).then_inc(acc_ready, 1)
                counts["acc"].next()

            def clear_acc():
                nc.vector.memset(acc[:, :], 0.0).then_inc(acc_ready, 1)
                counts["acc"].next()

            def inverse_root(by_token):
                dve.wait_ge(side_done[0], counts["side0"].next())
                if by_token:
                    nc.vector.tensor_scalar(norm_cols, side[0][:, S:S + 2 * TILES], 1.0 / D, EPS, ALU.mult, ALU.add)
                side_out(0, nc.vector.tensor_scalar(rstd[:, :], side[0][:, 0:S], 1.0 / D, EPS, ALU.mult, ALU.add))
                dve.wait_ge(std_made, counts["std"].next())
                if by_token:
                    nc.vector.reciprocal(norm_cols, norm_cols)
                nc.vector.reciprocal(rstd[:, :], rstd[:, :]).then_inc(rstd_made, 1)
                dve.wait_ge(rstd_made, counts["rstd"].next())

            def ffn(gain, last):
                def inner(i, first=False, k_next=UNIT_K):
                    split()
                    if first:
                        inverse_root(False)
                    done()
                    evac(0, scaled(two(gs[:, :]), 0))
                    step(k_next)
                    v_ = evac(1, scaled(two(us[:, :]), 1))
                    dve.wait_ge(evacuated[1], v_)
                    dve.wait_ge(silu_made, counts["silu"].next())
                    nc.vector.tensor_tensor(us[:, :], us[:, :], gs[:, :], ALU.mult).then_inc(act_made, 1)
                    dve.wait_ge(act_hi_made, counts["act_hi"].next())
                    nc.vector.tensor_tensor(pair(act_lo, i), us[:, :], pair(act_hi, i).bitcast(F32),
                                            ALU.subtract).then_inc(act_ready, 1)
                inner(0, True)
                with rounds(dve, FF_UNITS - 2, counts, unit=2, hi=2, ev0=1, ev1=1, silu=1, act_hi=1) as i:
                    inner(i + 1)
                inner(FF_UNITS - 1, k_next=DOWN_K[0][1])
                clear_acc()
                widths = [k1 - k0 for k0, k1 in DOWN_K]
                for d in range(D_PAIRS):
                    for n in range(3):
                        end = d == D_PAIRS - 1 and n == 2
                        if not (end and last):
                            split(UNIT_K if end else widths[(n + 1) % 3])
                        done()
                    residual(0.5, gain, d, d % 2)

            handed = 100
            for s_, n in ((evacuated[0], 1), (evacuated[1], 1), (side_evacuated[0], 1), (side_evacuated[1], 1),
                          (split_made, 2), (unit_done, 2), (head_made, 2)):
                for _ in range(n):
                    nc.vector.memset(small[:, handed:handed + 1], 0.0).then_inc(s_, 1)
                    handed += 1
            for i in range(PAD):
                nc.vector.memset(inv_count[:, i:i + 1], 1.0 / (i + 1))
            clear_acc()

            dve.wait_ge(mask_step, MASK_STEPS)
            chain(nc.vector.tensor_scalar(index_i[:, :], index_i[:, :], 3, None, ALU.bitwise_and))
            chain(nc.vector.tensor_scalar(index_f[:, :], index_i[:, :], 0.5, MASKED, ALU.is_gt, ALU.mult))
            for r in range(RES):
                m2 = mask_f[:, r * KEYS + S + P:(r + 1) * KEYS]
                nc.vector.tensor_tensor(m2, m2, index_f[:, :], ALU.min).then_inc(dve_step, 1)
            dve.wait_ge(dve_step, counts["step"].next(RES))
            chain(nc.vector.tensor_copy(masks[:, :], mask_f[:, :]))

            dve.wait_ge(side_evacuated[1], counts["se1"].next())
            counts["side1"].next()
            for d in range(D_PAIRS):
                dve.wait_ge(turned, d + 1)
                residual(None, T_FFN1, d, d % 2)

            chained = sum(w.bit_length() for w in POOL_WINDOWS) + 5 + D_PAIRS + ATT
            with rounds(dve, DEPTH, counts, unit=UNITS_PER_LAYER, hi=UNITS_PER_LAYER, ev0=48 + ATT // 2, ev1=48 + ATT // 2, step=chained,
                        h_hi=12, sq=12, acc=15, side0=5 + ATT, side1=3, se0=5 + ATT, se1=3, std=3, rstd=3, silu=2 * FF_UNITS,
                        act_hi=2 * FF_UNITS, gelu=2, ln_std=1, yc_hi=2, yb_hi=2, y=2, pooled=KB, exp=ATT,
                        head=ATT, gate=3 * D_PAIRS, merged=D_PAIRS) as layer:
                split()
                ffn(layer * KD + T_MIX, False)

                def pool_sums(g):
                    w = POOL_WINDOWS[g]
                    c = c_pad[:, g * CP:(g + 1) * CP]
                    cur, shift, b = c, 1, 0
                    while shift < w:
                        nxt = sums[b]
                        chain(nc.vector.tensor_tensor(nxt[:, PAD:CP], cur[:, PAD:CP], cur[:, PAD - shift:CP - shift], ALU.add))
                        cur, shift, b = nxt, 2 * shift, 1 - b
                    chain(nc.vector.tensor_tensor(pool_head[:, 0:w - 1], cur[:, PAD:PAD + w - 1], inv_count[:, 0:w - 1], ALU.mult))
                    nc.vector.tensor_tensor(c[:, PAD:PAD + w - 1], pool_head[:, 0:w - 1], c[:, PAD:PAD + w - 1],
                                            ALU.subtract)
                    nc.vector.scalar_tensor_tensor(c[:, PAD + w - 1:CP], cur[:, PAD + w - 1:CP], 1.0 / w,
                                                   c[:, PAD + w - 1:CP], ALU.mult, ALU.subtract).then_inc(pooled, 1)
                    dve.wait_ge(pooled, counts["pooled"].next())

                def yc_lo_part(s):
                    dve.wait_ge(yc_hi_made, counts["yc_hi"].next())
                    for c in range(2):
                        g = 2 * s + c
                        i_ = nc.vector.scalar_tensor_tensor(yc_lo[:, g * S:(g + 1) * S], side[s][:, c * S:(c + 1) * S],
                                                            table[:, bass.ds(T_CSCALE + layer * KB + g, 1)],
                                                            yc_hi[:, g * S:(g + 1) * S].bitcast(F32), ALU.mult, ALU.subtract)
                    side_out(s, i_)

                for u in range(2):
                    split()
                    if u == 0:
                        inverse_root(True)
                        for i in range(4):
                            nc.vector.memset(c_pad[:, i * CP:i * CP + PAD], 0.0)
                        for s in range(2):
                            nc.vector.memset(sums[s][:, 0:PAD], 0.0)
                    done()
                    c2 = c_pad[:, 2 * u * CP:2 * (u + 1) * CP].rearrange("p (c s) -> p c s", s=CP)[:, :, PAD:CP]
                    v_ = evac(u, scaled(c2, u))
                    dve.wait_ge(evacuated[u], v_)
                    for c in range(2):
                        pool_sums(2 * u + c)
                for u in range(2):
                    step()
                    evac(u, scaled(two(pair(ub, u)), u))
                    if u == 1:
                        counts["side1"].next()
                        counts["se1"].next()
                    yc_lo_part(u)
                    counts[f"side{u}"].next()
                for u in range(2):
                    split(UNIT_K, UNIT_N if u == 0 else V_N)
                    counts["unit"].next()
                    counts[f"ev{u}"].next()
                for u in range(2):
                    dve.wait_ge(evacuated[u], counts[f"ev{u}"].now())
                for t in range(TILES):
                    i_ = nc.vector.bn_stats(ln_stats[:, 6 * t:6 * t + 6], vb[:, t * BW:(t + 1) * BW])
                chain(i_)
                nc.vector.memset(small[:, 126:127], 0.0)
                for t in range(TILES):
                    i_ = nc.vector.bn_aggr(ln_mv[:, 2 * t:2 * t + 2], ln_stats[:, 6 * t:6 * t + 6])
                chain(i_)
                var = ln_mv.rearrange("p (t c) -> p t c", c=2)[:, :, 1]
                nc.vector.tensor_scalar(ln_rs, var, EPS, None, ALU.add).then_inc(ln_var_made, 1)
                dve.wait_ge(ln_std_made, counts["ln_std"].next())
                chain(nc.vector.reciprocal(ln_rs, ln_rs))
                for t in range(TILES):
                    i_ = nc.vector.tensor_scalar(vb[:, t * BW:(t + 1) * BW], vb[:, t * BW:(t + 1) * BW],
                                                 ln_mv[:, 2 * t:2 * t + 1], ln_rs[:, t:t + 1], ALU.subtract, ALU.mult)
                chain(i_)
                vb4 = vb[:, :].rearrange("p (t c) -> p t c", c=BW)
                dve.wait_ge(params_loaded, 16 * 5 + layer * (16 * 5))
                chain(nc.vector.tensor_tensor(vb4, vb4, ln_g[:, :].unsqueeze(1).broadcast_to([P, TILES, BW]), ALU.mult))
                nc.vector.tensor_tensor(vb4, vb4, ln_b[:, :].unsqueeze(1).broadcast_to([P, TILES, BW]),
                                        ALU.add).then_inc(vb_ready, 1)

                def gating(s):
                    dve.wait_ge(side_done[s], counts[f"side{s}"].next())
                    if s == 0:
                        dve.wait_ge(gelu_made, counts["gelu"].next(2))
                    g4 = gs[:, :].rearrange("p (g b t) -> p g b t", g=2, t=CHUNK)
                    v_ = side_out(s, nc.vector.tensor_tensor(
                        g4, side[s][:, :].rearrange("p (g b t) -> p g b t", g=2, t=CHUNK),
                        bias_s[:, 2 * s * CHUNK:2 * (s + 1) * CHUNK].rearrange("p (g t) -> p g t", t=CHUNK)
                        .unsqueeze(2).broadcast_to([P, 2, TILES, CHUNK]), ALU.add))
                    dve.wait_ge(side_evacuated[s], v_)
                    nc.vector.tensor_tensor(gs[:, :], gs[:, :], pair(ub, s), ALU.mult).then_inc(yb_made, 1)
                    dve.wait_ge(yb_hi_made, counts["yb_hi"].next())
                    nc.vector.tensor_tensor(pair(yb_lo, s), gs[:, :], pair(yb_hi, s).bitcast(F32),
                                            ALU.subtract).then_inc(y_ready, 1)
                    dve.wait_ge(y_ready, counts["y"].next())
                for u in range(4):
                    split(UNIT_K, V_N if u < 3 else UNIT_N)
                    counts["unit"].next()
                    counts[f"ev{u % 2}"].next()
                    if u >= 2:
                        gating(u - 2)
                rstd_i = rstd[:, :].rearrange("p (i r) -> p i r", r=RES)
                for u in range(2 * GROUPS):
                    step()
                    g = u % GROUPS
                    dst = (qT if u < GROUPS else kT)
                    for c in range(2):
                        d_ = dst[:, (2 * g + c) * S:(2 * g + c + 1) * S].rearrange("p (r i) -> p i r", r=RES)
                        s_ = psum[u % 2][:, c * S:(c + 1) * S].rearrange("p (i r) -> p i r", r=RES)
                        i_ = nc.vector.scalar_tensor_tensor(d_, s_, HEAD_DIM ** -0.5 if u < GROUPS else 1.0, rstd_i,
                                                            ALU.mult, ALU.mult)
                    evac(u % 2, i_)

                def head_lo(n):
                    j, r = divmod(n, RES)
                    rows_ = slice((j % 2) * HEAD_DIM, (j % 2 + 1) * HEAD_DIM)
                    dve.wait_ge(ya_hi_made, counts["head"].next())
                    a = slice((j // 2) * S, (j // 2 + 1) * S)
                    nc.vector.tensor_tensor(ya_lo[rows_, a].rearrange("p (i r) -> p r i", r=RES)[:, r, :],
                                            side[1][rows_, (n % 2) * S:(n % 2) * S + P],
                                            ya_hi[rows_, a].rearrange("p (i r) -> p r i", r=RES)[:, r, :].bitcast(F32),
                                            ALU.subtract).then_inc(head_made, 1)

                def score_max(n):
                    dve.wait_ge(side_done[0], counts["side0"].next())
                    b = slice(n % 2, n % 2 + 1)
                    r = n % RES
                    nc.vector.memset(small[:, 126:127], 0.0)
                    v_ = side_out(0, nc.vector.tensor_tensor_reduce(
                        p_tile[n % 2][:, :], side[0][:, 0:KEYS], masks[:, r * KEYS:(r + 1) * KEYS],
                        1.0, 3 * MASKED, ALU.add, ALU.max, row_max[:, b]))
                    dve.wait_ge(side_evacuated[0], v_)
                    nc.vector.tensor_scalar(neg_max[:, b], row_max[:, b], -1.0, None, ALU.mult).then_inc(neg_max_made, 1)

                score_max(0)
                for n in range(ATT):
                    b = slice(n % 2, n % 2 + 1)
                    dve.wait_ge(exp_made, counts["exp"].next())
                    chain(nc.vector.reciprocal(row_inv[:, b], row_sum[:, b]))
                    nc.vector.tensor_scalar(p_tile[n % 2][:, :], p_tile[n % 2][:, :], row_inv[:, b], None,
                                            ALU.mult).then_inc(p_made, 1)
                    if n > 0:
                        head_lo(n - 1)
                    if n + 1 < ATT:
                        score_max(n + 1)
                head_lo(ATT - 1)
                for s in range(2):
                    counts[f"ev{s}"].next(ATT // 2)

                with rounds(dve, D_PAIRS // 2, counts, unit=10, hi=10, ev0=6, ev1=6, step=2, gate=6, merged=2) as half:
                    for d in range(2):
                        for g in range(3):
                            step(UNIT_K if g < 2 else KA + KB)
                            evac(g % 2, scaled(two(gate[g][:, :]), g % 2))
                        step(KB)
                        dve.wait_ge(gate_made, counts["gate"].next(3))
                        va = evac(1, nc.vector.tensor_tensor(gate[0][:, :], gate[0][:, :], psum[1][:, :], ALU.mult))
                        vb_ = evac(0, nc.vector.tensor_tensor(gate[1][:, :], gate[1][:, :], psum[0][:, :], ALU.mult))
                        dve.wait_ge(evacuated[1], va)
                        dve.wait_ge(evacuated[0], vb_)
                        chain(nc.vector.tensor_tensor(gate[0][:, :], gate[0][:, :], gate[1][:, :], ALU.add))
                        step()
                        vc = evac(1, nc.vector.tensor_tensor(gate[2][:, :], gate[2][:, :], psum[1][:, :], ALU.mult))
                        dve.wait_ge(evacuated[1], vc)
                        nc.vector.tensor_tensor(gate[0][:, :], gate[0][:, :], gate[2][:, :], ALU.add).then_inc(merged_made, 1)
                        dve.wait_ge(merged_hi_made, counts["merged"].next())
                        nc.vector.tensor_tensor(pair(m_lo, half * 2 + d), gate[0][:, :],
                                                pair(m_hi, half * 2 + d).bitcast(F32), ALU.subtract).then_inc(merged_ready, 1)
                        dve.wait_ge(merged_ready, counts["merged"].now())
                clear_acc()
                with rounds(dve, D_PAIRS // 2, counts, unit=2, hi=2, ev0=1, ev1=1, h_hi=2, sq=2, acc=2) as half:
                    for d in range(2):
                        step()
                        residual(1.0, layer * KD + T_FFN2, half * 2 + d, d)
                ffn(layer * KD + (T_FFN1 + KD), True)

            dve.wait_ge(side_done[0], counts["side0"].next())
            nc.vector.tensor_scalar(norm_cols, side[0][:, 0:2 * TILES], 1.0 / D, EPS, ALU.mult, ALU.add).then_inc(side_evacuated[0], 1)
            dve.wait_ge(std_made, counts["std"].next())
            chain(nc.vector.reciprocal(norm_cols, norm_cols))
            dve.wait_ge(gains_loaded, 16)
            for t in range(TILES):
                dve.wait_ge(turned, D_PAIRS + t + 1)
                nc.vector.scalar_tensor_tensor(x_out[:, t * D:(t + 1) * D], psum[t % 2][:, :], norm_cols[:, t:t + 1],
                                               gain_rows[:, :], ALU.mult, ALU.mult).then_inc(out_made, 1)



_INS = ["x", "ffn1_norm", "ffn1_w_gate", "ffn1_w_up", "ffn1_w_down", "mix_norm", "w_in", "b_gate", "b_ln_g",
        "b_ln_b", "b_w_s", "b_b_s", "c_w", "c_scale", "w_proj_a", "w_proj_b", "w_proj_c", "w_out", "ffn2_norm",
        "ffn2_w_gate", "ffn2_w_up", "ffn2_w_down", "final_norm"]


def kernel(**inputs):
    import numpy as _np
    import concourse.bacc as _bacc
    from concourse import mybir as _mybir
    from concourse.bass_utils import run_bass_kernel_spmd as _run

    nc = _bacc.Bacc("TRN2", target_bir_lowering=False, num_devices=1)
    arrays, args = {}, []
    for name in _INS:
        a = _np.ascontiguousarray(inputs[name])
        arrays[f"in_{name}_dram"] = a
        args.append(nc.dram_tensor(f"in_{name}_dram", a.shape, _mybir.dt.from_np(a.dtype), kind="ExternalInput").ap())
    shape = inputs["x"].shape
    out = nc.dram_tensor("out_0_dram", shape, _mybir.dt.float32, kind="ExternalOutput").ap()
    trunk(nc, *args, out)
    r = _run(nc, [arrays], core_ids=[0])
    return r.results[0]["out_0_dram"]
```

```python
from contextlib import ExitStack, contextmanager

import concourse.bass as bass
from concourse import mybir

F32 = mybir.dt.float32
F32R = mybir.dt.float32r
BF16 = mybir.dt.bfloat16
I32 = mybir.dt.int32
ALU = mybir.AluOpType
ACT = mybir.ActivationFunctionType

P = 128
EPS = 1e-6
HEAD_DIM = 64
HEADS = 4
GROUPS = 3
WINDOW0 = 128
RES = 4
CHUNK = 128
POOL_WINDOWS = (2, 4, 8, 16)
PAD = 16
MASKED = -1e30
UNIT_K = 8
UNIT_N = 256


class Count:

    def __init__(self, start=0):
        self.base, self.local, self.outer = start, 0, []

    def next(self, n=1):
        self.local += n
        return self.base + self.local

    def now(self, more=0):
        return self.base + (self.local + more)

    def enter(self, i, per):
        self.outer.append((self.base, self.local))
        self.base, self.local = self.base + self.local + i * per, 0

    def leave(self, rounds, per):
        base, local = self.outer.pop()
        self.base, self.local = base, local + rounds * per


@contextmanager
def rounds(eng, n, counts, **per):
    with eng.Fori(0, n) as i:
        for name, c in counts.items():
            c.enter(i, per.get(name, 0))
        yield i
        wrong = {name: c.local for name, c in counts.items() if c.local != per.get(name, 0)}
        assert not wrong, wrong
    for name, c in counts.items():
        c.leave(n, per.get(name, 0))


def trunk(nc, x, ffn1_norm, ffn1_w_gate, ffn1_w_up, ffn1_w_down, mix_norm, w_in, b_gate, b_ln_g,
          b_ln_b, b_w_s, b_b_s, c_w, c_scale, w_proj_a, w_proj_b, w_proj_c, w_out, ffn2_norm,
          ffn2_w_gate, ffn2_w_up, ffn2_w_down, final_norm, out):
    DEPTH, D, FF = ffn1_w_gate.shape
    S = x.shape[1]
    KD = D // P
    KF = FF // P
    FF_UNITS = FF // UNIT_N
    D_PAIRS = D // UNIT_N
    TILES = S // P
    A_OUT = HEADS * HEAD_DIM
    A_WIDTH = GROUPS * A_OUT
    BW = b_ln_g.shape[1]
    KA, KB = A_OUT // P, BW // P
    Q_OFF, K_OFF, V_OFF = 0, A_WIDTH, 2 * A_WIDTH
    UB_OFF = 3 * A_WIDTH
    VB_OFF, C_OFF, G_OFF = UB_OFF + BW, UB_OFF + 2 * BW, UB_OFF + 3 * BW
    ATT = HEADS * RES
    KEYS = S + 2 * P
    QK_UNITS = ((0, 1), (2, 3), (4, 5))
    UNITS_PER_LAYER = 2 * (2 * FF_UNITS + D_PAIRS * 3) + 6 + GROUPS + 7 + 6 * D_PAIRS + D_PAIRS
    EV0, EV1 = 48, 47
    DOWN_K = [(k, min(k + UNIT_K, KF)) for k in range(0, KF, UNIT_K)]
    assert (S, D, TILES, RES, KD) == (4 * P, 8 * P, 4, 4, 8) and len(DOWN_K) == 3 and UNITS_PER_LAYER % 2 == 0
    assert FF % UNIT_N == 0 and D_PAIRS == 4 and BW == 2 * UNIT_N == S

    with ExitStack() as ctx:
        base = 16512
        def at(name, offset, cols, dt=F32):
            return nc.alloc_sbuf_tensor_at(name, [P, cols], dt, offset=base + offset)

        KB_ = 1024
        xT = at("xT", 0, KD * S)
        h_hi = at("h_hi", 16 * KB_, KD * S, F32R)
        h_lo = at("h_lo", 32 * KB_, KD * S, F32R)
        raw = [at(f"raw{s}", (48 + 8 * s) * KB_, UNIT_K * UNIT_N) for s in range(2)]
        w_hi = [at(f"w_hi{s}", (64 + 16 * s) * KB_, UNIT_K * UNIT_N, F32R) for s in range(2)]
        w_lo = [at(f"w_lo{s}", (72 + 16 * s) * KB_, UNIT_K * UNIT_N, F32R) for s in range(2)]
        rstd = at("rstd", 96 * KB_, S)
        acc = at("acc", 98 * KB_, 2 * S)
        gs = at("gs", 102 * KB_, 2 * S)
        us = at("us", 106 * KB_, 2 * S)
        masks = at("masks", 110 * KB_, RES * KEYS, BF16)
        ident = at("ident", 116 * KB_, P)
        ones = at("ones", 116 * KB_ + 512, P)
        table = at("table", 117 * KB_, P)
        small = at("small", 117 * KB_ + 512, P)
        M = 118 * KB_
        act_hi = at("act_hi", M, KF * S, F32R)
        act_lo = at("act_lo", M + KF * S * 4, KF * S, F32R)
        x_in = at("x_in", M, TILES * D)
        vectors = at("vectors", M + 16 * KB_, P)
        x_out = at("x_out", M, TILES * D)
        gain_rows = at("gain_rows", M + 16 * KB_, D)
        vb = at("vb", M, TILES * BW)
        w_s = at("w_s", M + 8 * KB_, KB * CHUNK)
        bias_s = at("bias_s", M + 10 * KB_, KB * CHUNK)
        ln_g = at("ln_g", M + 12 * KB_, BW)
        ln_b = at("ln_b", M + 14 * KB_, BW)
        cw = at("cw", M + 16 * KB_, KB * P)
        w_sT = at("w_sT", M + 18 * KB_, KB * CHUNK)
        CP = PAD + S
        c_pad = at("c_pad", M + 24 * KB_, 4 * CP)
        sums = [at(f"sums{s}", M + 36 * KB_ + s * 3 * KB_, CP) for s in range(2)]
        qk = [at(f"qk{s}", M + 12 * s * KB_, 6 * S) for s in range(2)]
        v = at("v", M + 24 * KB_, TILES * A_WIDTH)
        p_tile = [at(f"p_tile{s}", M + 36 * KB_ + s * 3 * KB_, KEYS) for s in range(2)]
        pT = at("pT", M + 42 * KB_, KEYS)
        ya_hi = at("ya_hi", M + 45 * KB_, KA * S, F32R)
        ya_lo = at("ya_lo", M + 49 * KB_, KA * S, F32R)
        ub = at("ub", M + 53 * KB_, KB * S)
        yb_hi = at("yb_hi", M + 53 * KB_, KB * S, F32R)
        yb_lo = at("yb_lo", M + 61 * KB_, KB * S, F32R)
        yc_hi = at("yc_hi", M + 69 * KB_, KB * S, F32R)
        yc_lo = at("yc_lo", M + 77 * KB_, KB * S, F32R)
        gate = [at(f"gate{g}", M + 4 * g * KB_, 2 * S) for g in range(3)]
        m_hi = at("m_hi", M + 12 * KB_, KD * S, F32R)
        m_lo = at("m_lo", M + 28 * KB_, KD * S, F32R)

        norm_cols = small[:, 0:8]
        ln_stats = small[:, 8:32]
        ln_mv = small[:, 32:40]
        ln_rs = small[:, 40:44]
        neg_max = small[:, 44:46]
        row_max = small[:, 46:48]
        row_sum = small[:, 48:50]
        row_inv = small[:, 50:52]
        inv_count = small[:, 64:64 + PAD]
        pool_head = small[:, 80:80 + PAD]
        T_FFN1, T_MIX, T_FFN2, T_FINAL = 0, DEPTH * KD, 2 * DEPTH * KD, 3 * DEPTH * KD
        T_BGATE = T_FINAL + KD
        T_CSCALE = T_BGATE + DEPTH * 3 * KD
        N_VEC = T_CSCALE + DEPTH * KB
        assert N_VEC <= P

        psum = [ctx.enter_context(nc.psum_tensor(f"psum{s}", [P, 2 * S], F32)) for s in range(2)]
        side = [ctx.enter_context(nc.psum_tensor(f"side{s}", [P, 2 * S], F32)) for s in range(2)]

        def sem(name):
            return ctx.enter_context(nc.semaphore(name))

        x_loaded = sem("x_loaded")
        vectors_loaded = sem("vectors_loaded")
        params_loaded = sem("params_loaded")
        gains_loaded = sem("gains_loaded")
        stored = sem("stored")
        consts_made = sem("consts_made")
        mask_step = sem("mask_step")
        table_made = sem("table_made")
        raw_loaded = [sem(f"raw_loaded{s}") for s in range(2)]
        hi_made = sem("hi_made")
        split_made = sem("split_made")
        unit_done = sem("unit_done")
        evacuated = [sem(f"evacuated{s}") for s in range(2)]
        side_done = [sem(f"side_done{s}") for s in range(2)]
        side_evacuated = [sem(f"side_evacuated{s}") for s in range(2)]
        h_hi_made = sem("h_hi_made")
        sq_made = sem("sq_made")
        h_ready = sem("h_ready")
        acc_ready = sem("acc_ready")
        std_made = sem("std_made")
        rstd_made = sem("rstd_made")
        silu_made = sem("silu_made")
        act_made = sem("act_made")
        act_hi_made = sem("act_hi_made")
        act_ready = sem("act_ready")
        w_sT_made = sem("w_sT_made")
        pooled = sem("pooled")
        yc_hi_made = sem("yc_hi_made")
        gelu_made = sem("gelu_made")
        ln_var_made = sem("ln_var_made")
        ln_std_made = sem("ln_std_made")
        vb_ready = sem("vb_ready")
        yb_made = sem("yb_made")
        yb_hi_made = sem("yb_hi_made")
        neg_max_made = sem("neg_max_made")
        exp_made = sem("exp_made")
        p_made = sem("p_made")
        pT_written = sem("pT_written")
        pT_made = sem("pT_made")
        head_done = sem("head_done")
        ya_hi_made = sem("ya_hi_made")
        head_made = sem("head_made")
        y_ready = sem("y_ready")
        gate_made = sem("gate_made")
        merged_made = sem("merged_made")
        merged_hi_made = sem("merged_hi_made")
        merged_ready = sem("merged_ready")
        dve_step = sem("dve_step")
        turned = sem("turned")
        out_made = sem("out_made")

        block = ctx.enter_context(nc.Block())

        SLOTS = 18
        MASK_STEPS = 1 + P // RES + (RES - 1) + 3 * RES

        def attended(s):
            if s in (0, 9) or not 0 < s < SLOTS:
                return None
            return s - 1 if s < 9 else s - 2

        def pair(t, d, n=2 * S):
            return t[:, bass.ds(d * (2 * S), n)]

        @block.sync
        def _(sp):
            counts = dict(split_made=Count())

            def load(parts):
                slot = load.slot
                sp.wait_ge(split_made, counts["split_made"].next())
                n = sum(src.shape[2] for src in parts)
                dst = raw[slot][:, 0:UNIT_K * n].rearrange("p (k n) -> p k n", n=n)
                for c, src in reversed(list(enumerate(parts))):
                    w = src.shape[2]
                    sp.dma_start(dst[:, 0:src.shape[1], c * w:(c + 1) * w], src).then_inc(raw_loaded[slot], 16)
                load.slot = 1 - slot
            load.slot = 0

            def view(w, layer, col, n, k0=0, k1=None):
                src = w[bass.ds(layer, 1)].rearrange("a (k p) n -> p (a k) n", p=P)
                return src[:, k0:k1 or src.shape[1], bass.ds(col, n)]

            def load_ffn(layer, w_gate, w_up, w_down):
                with rounds(sp, FF_UNITS, counts, split_made=2) as i:
                    for w in (w_gate, w_up):
                        load([view(w, layer, i * UNIT_N, UNIT_N)])
                with rounds(sp, D_PAIRS // 2, counts, split_made=2 * len(DOWN_K)) as half:
                    for d in range(2):
                        for k0, k1 in DOWN_K:
                            load([view(w_down, layer, half * (2 * UNIT_N) + d * UNIT_N, UNIT_N, k0, k1)])

            with rounds(sp, DEPTH, counts, split_made=UNITS_PER_LAYER) as layer:
                load_ffn(layer, ffn1_w_gate, ffn1_w_up, ffn1_w_down)
                for off in (C_OFF, UB_OFF, VB_OFF):
                    for u in range(2):
                        load([view(w_in, layer, off + u * UNIT_N, UNIT_N)])
                for u in range(GROUPS):
                    load([view(w_in, layer, V_OFF + u * UNIT_N, UNIT_N)])
                for jp in range(2):
                    for a in QK_UNITS:
                        views = [view(w_in, layer, (Q_OFF if c < GROUPS else K_OFF) + (c % GROUPS) * A_OUT + jp * P, P)
                                 for c in a]
                        if jp == 0 and a == QK_UNITS[2]:
                            load(views[0:1])
                            load(views[1:2])
                        else:
                            load(views)

                def load_merge(col):
                    for g in range(3):
                        load([view(w_in, layer, G_OFF + g * D + col, UNIT_N)])
                    for w in (w_proj_a, w_proj_b, w_proj_c):
                        load([view(w, layer, col, UNIT_N)])
                load_merge(0)
                with rounds(sp, D_PAIRS - 1, counts, split_made=6) as i:
                    load_merge(i * UNIT_N + UNIT_N)
                with rounds(sp, D_PAIRS // 2, counts, split_made=2) as half:
                    for d in range(2):
                        load([view(w_out, layer, half * (2 * UNIT_N) + d * UNIT_N, UNIT_N)])
                load_ffn(layer, ffn2_w_gate, ffn2_w_up, ffn2_w_down)

            sp.wait_ge(unit_done, DEPTH * UNITS_PER_LAYER + 2)
            sp.dma_start(gain_rows[:, :], final_norm.partition_broadcast(P)).then_inc(gains_loaded, 16)
            for b in range(TILES):
                sp.wait_ge(out_made, b + 1)
                sp.dma_start(out[0, b * P:(b + 1) * P, :], x_out[:, b * D:(b + 1) * D]).then_inc(stored, 16)
            sp.wait_ge(stored, 16 * TILES)


        @block.gpsimd
        def _(pool):
            row = 0
            for vec in (ffn1_norm, mix_norm, ffn2_norm):
                for l in range(DEPTH):
                    pool.dma_start(vectors[row:row + KD, :], vec[l].rearrange("(k p) -> k p", p=P)) \
                      .then_inc(vectors_loaded, 16)
                    row += KD
            pool.dma_start(vectors[row:row + KD, :], final_norm.rearrange("(k p) -> k p", p=P)) \
              .then_inc(vectors_loaded, 16)
            row += KD
            for l in range(DEPTH):
                pool.dma_start(vectors[row:row + 3 * KD, :], b_gate[l].rearrange("(k p) -> k p", p=P)) \
                  .then_inc(vectors_loaded, 16)
                row += 3 * KD
            for l in range(DEPTH):
                pool.dma_start(vectors[row:row + KB, :], c_scale[l]).then_inc(vectors_loaded, 16)
                row += KB

            def fill(t, c):
                nc.gpsimd.memset(t, c).then_inc(consts_made, 1)
            fill(ident[:, :], 0.0)
            fill(ones[:, :], 1.0)
            fill(masks[:, :], 0.0)
            pool.wait_ge(consts_made, 3)
            nc.gpsimd.affine_select(out=ident[:, :], in_=ident[:, :], compare_op=ALU.not_equal, fill=1.0,
                                    base=0, pattern=[[-1, P]], channel_multiplier=1).then_inc(consts_made, 1)
            nc.gpsimd.memset(masks[:, S + P:KEYS], MASKED).then_inc(mask_step, 1)
            n = 1
            for d in range(0, P, RES):
                m2 = masks[:, S + P:KEYS]
                pool.wait_ge(mask_step, n)
                nc.gpsimd.affine_select(out=m2, in_=m2, compare_op=ALU.not_equal, fill=0.0, base=-d,
                                        pattern=[[-1, P]], channel_multiplier=1).then_inc(mask_step, 1)
                n += 1
            pool.wait_ge(mask_step, n)
            for r in range(1, RES):
                nc.gpsimd.tensor_copy(masks[:, r * KEYS + S + P:(r + 1) * KEYS], masks[:, S + P:KEYS]).then_inc(mask_step, 1)
                n += 1
            for r in range(RES):
                m0 = masks[:, r * KEYS:r * KEYS + S]
                for sign, base_ in ((1, r), (-1, WINDOW0 - r)):
                    nc.gpsimd.affine_select(out=m0, in_=m0, compare_op=ALU.is_ge, fill=MASKED, base=base_,
                                            pattern=[[-sign, RES], [-RES * sign, P]],
                                            channel_multiplier=RES * sign).then_inc(mask_step, 1)
                    n += 1
                    pool.wait_ge(mask_step, n)
                m1 = masks[:, r * KEYS + S:r * KEYS + S + P]
                nc.gpsimd.affine_select(out=m1, in_=m1, compare_op=ALU.is_ge, fill=MASKED, base=0,
                                        pattern=[[-1, P]], channel_multiplier=1).then_inc(mask_step, 1)
                n += 1
            assert n == MASK_STEPS
            for layer in range(DEPTH):
                pool.wait_ge(side_evacuated[1], 3 + layer * 3)
                nc.gpsimd.affine_select(out=w_sT[:, :], in_=w_sT[:, :], compare_op=ALU.is_ge, fill=0.0, base=0,
                                        pattern=[[0, KB], [1, CHUNK]], channel_multiplier=-1).then_inc(w_sT_made, 1)
        @block.tensor
        def _(pe):
            counts = {k: Count() for k in ("ev0", "ev1", "sv0", "sv1", "h", "acc", "act", "w_sT", "pooled",
                                           "vb", "p", "pT", "head", "y", "merged", "exp")}
            counts["unit"] = Count(2)
            pe_slot = [0]

            def begin(s):
                pe.wait_ge(evacuated[s], counts[f"ev{s}"].next())
                return psum[s]

            def begin_side(s):
                pe.wait_ge(side_evacuated[s], counts[f"sv{s}"].next())
                return side[s]

            def unit():
                pe.wait_ge(split_made, counts["unit"].next())
                slot = pe_slot[0]
                pe_slot[0] = 1 - slot
                return w_hi[slot], w_lo[slot]

            def columns(dst, w, x_hi, x_lo, ks, first, last, x_k0=0, need=None):
                whi, wlo = w
                order = [(c, k) for c in range(2) for k in ks]
                if need:
                    order = [(c, k) for part in (ks[:-2], ks[-2:]) for c in range(2) for k in part]
                for c, k in order:
                    o = dst[:, c * S:(c + 1) * S]
                    if c == 0 and need:
                        need(k)
                    if True:
                        a = slice(k * UNIT_N + c * P, k * UNIT_N + (c + 1) * P)
                        b = slice((x_k0 + k) * S, (x_k0 + k + 1) * S)
                        for n, (l, r) in enumerate(((whi, x_hi), (whi, x_lo), (wlo, x_hi))):
                            mm = nc.tensor.matmul(o, l[:, a], r[:, b], start=first and k == ks[0] and n == 0,
                                                  stop=last and k == ks[-1] and n == 2)
                return mm

            def part(dst, w, x_hi, x_lo, q0, q1):
                whi, wlo = w
                for q in range(q0, q1):
                    c, k, n = q // (3 * KD), q // 3 % KD, q % 3
                    l, r = ((whi, x_hi), (whi, x_lo), (wlo, x_hi))[n]
                    mm = nc.tensor.matmul(dst[:, c * S:(c + 1) * S], l[:, k * UNIT_N + c * P:k * UNIT_N + (c + 1) * P],
                                          r[:, k * S:(k + 1) * S], start=(k == 0 and n == 0), stop=(k == KD - 1 and n == 2))
                return mm

            def one_column(o, w):
                whi, wlo = w
                for k in range(KD):
                    for n, (l, r) in enumerate(((whi, h_hi), (whi, h_lo), (wlo, h_hi))):
                        mm = nc.tensor.matmul(o, l[:, k * P:(k + 1) * P], r[:, k * S:(k + 1) * S],
                                              start=(k == 0 and n == 0), stop=(k == KD - 1 and n == 2))
                return mm

            def need_h(k):
                if k % 2 == 0:
                    pe.wait_ge(h_ready, counts["h"].next())

            def norm_sums(by_token):
                pe.wait_ge(acc_ready, counts["acc"].next(1 + D_PAIRS))
                o = begin_side(0)
                for c in range(2):
                    mm = nc.tensor.matmul(o[:, 0:S], ones[:, :], acc[:, c * S:(c + 1) * S], start=(c == 0), stop=(c == 1))
                if by_token:
                    mm = token_sums(o, S)
                mm.then_inc(side_done[0], 1)

            def token_sums(o, at_col):
                for t in range(2 * TILES):
                    for c in range(2):
                        a = acc[:, c * S:(c + 1) * S]
                        a = a[:, t * P:(t + 1) * P] if t < TILES else \
                            a.rearrange("p (i r) -> p r i", r=RES)[:, t - TILES, :]
                        mm = nc.tensor.matmul(o[:, at_col + t:at_col + t + 1], a, ones[:, 0:1], start=(c == 0), stop=(c == 1))
                return mm

            def ffn():
                o = begin(0)
                columns(o, unit(), h_hi, h_lo, range(KD), True, True, need=need_h).then_inc(unit_done, 1)
                norm_sums(False)
                o = begin(1)
                columns(o, unit(), h_hi, h_lo, range(KD), True, True).then_inc(unit_done, 1)
                with rounds(pe, FF_UNITS - 1, counts, unit=2, ev0=1, ev1=1):
                    for s in range(2):
                        o = begin(s)
                        columns(o, unit(), h_hi, h_lo, range(KD), True, True).then_inc(unit_done, 1)
                counts["act"].next(FF_UNITS)
                with rounds(pe, D_PAIRS // 2, counts, unit=2 * len(DOWN_K), ev0=1, ev1=1):
                    for s in range(2):
                        o = begin(s)
                        for n, (k0, k1) in enumerate(DOWN_K):
                            pe.wait_ge(act_ready, counts["act"].now(k1 // 2 - FF_UNITS))
                            columns(o, unit(), act_hi, act_lo, range(k1 - k0), n == 0, n == len(DOWN_K) - 1,
                                    x_k0=k0).then_inc(unit_done, 1)

            pe.wait_ge(consts_made, 4)
            pe.wait_ge(vectors_loaded, 16 * (3 * DEPTH + 1 + 2 * DEPTH))
            o = begin_side(1)
            nc.tensor.transpose(o[:, 0:N_VEC], vectors[0:N_VEC, :], ident[0:N_VEC, 0:N_VEC]).then_inc(side_done[1], 1)
            pe.wait_ge(x_loaded, 16 * TILES)
            for d in range(D_PAIRS):
                o = begin(d % 2)
                for c in range(2):
                    for t in range(TILES):
                        mm = nc.tensor.transpose(o[:, c * S + t * P:c * S + (t + 1) * P],
                                                 x_in[:, t * D + (2 * d + c) * P:t * D + (2 * d + c + 1) * P], ident[:, :])
                mm.then_inc(turned, 1)

            with rounds(pe, DEPTH, counts, unit=UNITS_PER_LAYER, ev0=EV0, ev1=EV1,
                        sv0=3 + 2 + ATT, sv1=3, h=3 * D_PAIRS, acc=3 * (1 + D_PAIRS), act=2 * FF_UNITS, w_sT=1, pooled=4,
                        vb=1, p=ATT, pT=ATT, head=ATT, y=2, merged=D_PAIRS, exp=0) as layer:
                ffn()

                o = begin(0)
                columns(o, unit(), h_hi, h_lo, range(KD), True, True, need=need_h).then_inc(unit_done, 1)
                norm_sums(True)
                pe.wait_ge(head_made, counts["head"].now(1))
                pe.wait_ge(params_loaded, 16 * 5 + layer * (16 * 5))
                o = begin_side(1)
                for g in range(KB):
                    mm = nc.tensor.transpose(o[:, g * P:(g + 1) * P], w_s[:, g * P:(g + 1) * P], ident[:, :])
                mm.then_inc(side_done[1], 1)
                o = begin(1)
                columns(o, unit(), h_hi, h_lo, range(KD), True, True).then_inc(unit_done, 1)

                def pool_out(s):
                    pe.wait_ge(pooled, counts["pooled"].next(2))
                    o = begin_side(s)
                    for c in range(2):
                        g = 2 * s + c
                        mm = nc.tensor.matmul(o[:, c * S:(c + 1) * S], cw[:, g * P:(g + 1) * P],
                                              c_pad[:, g * CP + PAD:(g + 1) * CP], start=True, stop=True)
                    mm.then_inc(side_done[s], 1)

                for u in range(2):
                    o = begin(u)
                    columns(o, unit(), h_hi, h_lo, range(KD), True, True).then_inc(unit_done, 1)
                    pool_out(u)

                def rows(s, n, x_of):
                    o = begin(s)
                    whi, wlo = unit()
                    for t in range(TILES):
                        d = o[:, t * UNIT_N:t * UNIT_N + n]
                        for k in range(KD):
                            b = slice(k * n, (k + 1) * n)
                            for m, (l, r) in enumerate(((h_hi, whi), (h_lo, whi), (h_hi, wlo))):
                                mm = nc.tensor.matmul(d, x_of(l[:, k * S:(k + 1) * S], t), r[:, b],
                                                      start=(k == 0 and m == 0), stop=(k == KD - 1 and m == 2))
                    mm.then_inc(unit_done, 1)

                natural = lambda a, t: a[:, t * P:(t + 1) * P]
                residue = lambda a, t: a.rearrange("p (i r) -> p r i", r=RES)[:, t, :]
                for u in range(2):
                    rows(u, UNIT_N, natural)
                for u in range(GROUPS):
                    rows(u % 2, UNIT_N, residue)
                    if u > 0:
                        s = u - 1
                        if u == 1:
                            pe.wait_ge(w_sT_made, counts["w_sT"].next())
                            pe.wait_ge(vb_ready, counts["vb"].next())
                        o = begin_side(s)
                        for c in range(2):
                            g = 2 * s + c
                            for t in range(TILES):
                                mm = nc.tensor.matmul(o[:, c * S + t * P:c * S + (t + 1) * P],
                                                      vb[:, t * BW + g * P:t * BW + (g + 1) * P],
                                                      w_sT[:, g * P:(g + 1) * P], start=True, stop=True)
                        mm.then_inc(side_done[s], 1)

                for s in (1, 0):
                    columns(begin(s), unit(), h_hi, h_lo, range(KD), True, True).then_inc(unit_done, 1)
                o = begin(1)
                for c in range(2):
                    one_column(o[:, c * S:(c + 1) * S], unit()).then_inc(unit_done, 1)

                def scores(n):
                    j, r = divmod(n, RES)
                    rows_ = slice((j % 2) * HEAD_DIM, (j % 2 + 1) * HEAD_DIM)
                    t = qk[j // 2]
                    o = begin_side(0)
                    col = 0
                    for g in range(GROUPS):
                        q, k = g * S + r * P, (GROUPS + g) * S
                        keys = t[rows_, k:k + S] if g == 0 else t[rows_, k + r * P:k + (r + 1) * P]
                        width = S if g == 0 else P
                        mm = nc.tensor.matmul(o[:, col:col + width], t[rows_, q:q + P], keys, start=True, stop=True)
                        col += width
                    mm.then_inc(side_done[0], 1)

                def transposes(n):
                    pe.wait_ge(p_made, counts["p"].next())
                    pe.wait_ge(head_made, counts["head"].next())
                    for c in range(KEYS // P):
                        mm = nc.tensor.transpose(side[1][:, c * P:(c + 1) * P], p_tile[n % 2][:, c * P:(c + 1) * P], ident[:, :])
                    mm.then_inc(pT_written, 1)

                def values(n):
                    j, r = divmod(n, RES)
                    pe.wait_ge(pT_made, counts["pT"].next())
                    out_rows = slice((j % 2) * HEAD_DIM, (j % 2 + 1) * HEAD_DIM)
                    o = side[1][out_rows, KEYS:KEYS + P]
                    for c in range(KEYS // P):
                        g, t = (0, c) if c < TILES else (c - TILES + 1, r)
                        col = t * A_WIDTH + g * A_OUT + j * HEAD_DIM
                        mm = nc.tensor.matmul(o, v[:, col:col + HEAD_DIM], pT[:, c * P:(c + 1) * P],
                                              start=(c == 0), stop=(c == KEYS // P - 1))
                    mm.then_inc(head_done, 1)

                pair_of = (0, 1, 0, 1, 0, 1)
                STEP = 3 * 2 * KD // 6
                for s in range(SLOTS):
                    m, third = divmod(s, 3)
                    this, after = attended(s), attended(s + 1)
                    if third == 0:
                        o = begin(pair_of[m])
                        w = unit()
                    if this is not None and after is not None:
                        scores(after)
                    start, end = 2 * STEP * third, 2 * STEP * (third + 1)
                    before, between = (STEP, STEP) if s < SLOTS - 1 else (STEP // 2, STEP - 2)
                    part(o, w, h_hi, h_lo, start, start + before)
                    if this is None:
                        if s == 0:
                            pe.wait_ge(side_evacuated[1], counts["sv1"].now(1))
                        pe.wait_ge(evacuated[1 - pair_of[m]], counts[f"ev{1 - pair_of[m]}"].now(1))
                        scores(after)
                    else:
                        transposes(this)
                    mm = part(o, w, h_hi, h_lo, start + before, start + before + between)
                    if third == 2 and s < SLOTS - 1:
                        mm.then_inc(unit_done, 1)
                    if this is not None:
                        values(this)
                part(o, w, h_hi, h_lo, start + before + between, end).then_inc(unit_done, 1)

                def project():
                    columns(begin(0), unit(), ya_hi, ya_lo, range(KA), True, True).then_inc(unit_done, 1)
                    columns(begin(1), unit(), yb_hi, yb_lo, range(KB), True, True).then_inc(unit_done, 1)
                    columns(begin(0), unit(), yc_hi, yc_lo, range(KB), True, True).then_inc(unit_done, 1)
                pe.wait_ge(head_made, counts["head"].now(1))
                pe.wait_ge(y_ready, counts["y"].next(2))
                project()
                with rounds(pe, D_PAIRS - 1, counts, unit=6, ev0=3, ev1=3):
                    for s in (1, 0, 1):
                        columns(begin(s), unit(), h_hi, h_lo, range(KD), True, True).then_inc(unit_done, 1)
                    project()
                counts["merged"].next(D_PAIRS)

                def need_merged(k):
                    if k % 2 == 0:
                        pe.wait_ge(merged_ready, counts["merged"].now(k // 2 + 1 - D_PAIRS))
                with rounds(pe, D_PAIRS // 2, counts, unit=2, ev0=1, ev1=1):
                    for s in range(2):
                        columns(begin(s), unit(), m_hi, m_lo, range(KD), True, True, need=need_merged).then_inc(unit_done, 1)
                ffn()

            pe.wait_ge(acc_ready, counts["acc"].next(1 + D_PAIRS))
            o = begin_side(0)
            token_sums(o, 0).then_inc(side_done[0], 1)
            for t in range(TILES):
                o = begin(t) if t < 2 else begin_side(1) if t == 2 else psum[0]
                if t == 3:
                    pe.wait_ge(out_made, 1)
                for k in range(KD):
                    mm = nc.tensor.transpose(o[:, k * P:(k + 1) * P], xT[:, k * S + t * P:k * S + (t + 1) * P], ident[:, :])
                mm.then_inc(turned, 1)

        @block.scalar
        def _(act):
            counts = {k: Count(1) for k in ("ev0", "ev1", "se0")}
            counts |= {k: Count() for k in ("unit", "raw0", "raw1", "act", "sd0", "sd1", "ln", "yb", "neg",
                                            "pT_written", "head", "merged")}
            slot = [0]

            def split(k=UNIT_K, n=UNIT_N, parts=1):
                s = slot[0]
                slot[0] = 1 - s
                act.wait_ge(raw_loaded[s], counts[f"raw{s}"].next(16 * parts))
                act.wait_ge(unit_done, counts["unit"].now(2))
                nc.scalar.activation(w_hi[s][:, 0:k * n], raw[s][:, 0:k * n], ACT.Copy).then_inc(hi_made, 1)

            def residual(layer, gain, d, s, sq=us):
                act.wait_ge(evacuated[s], counts[f"ev{s}"].next())
                for c in range(2):
                    a = bass.ds(d * (2 * S) + c * S, S)
                    mm = nc.scalar.activation(h_hi[:, a], xT[:, a], ACT.Copy,
                                              scale=table[:, bass.ds(gain + 2 * d + c, 1)])
                mm.then_inc(h_hi_made, 1)
                nc.scalar.activation(sq[:, :], pair(xT, d), ACT.Square).then_inc(sq_made, 1)

            def root(cols=None):
                counts["sd0"].next()
                act.wait_ge(side_evacuated[0], counts["se0"].next())
                if cols is not None:
                    nc.scalar.activation(cols, cols, ACT.Sqrt)
                nc.scalar.activation(rstd[:, :], rstd[:, :], ACT.Sqrt).then_inc(std_made, 1)

            def step(k=UNIT_K, n=UNIT_N, parts=1):
                split(k, n, parts)
                counts["unit"].next()

            widths = [k1 - k0 for k0, k1 in DOWN_K]

            def ffn(layer, gain, last):
                def inner(first, k_next=UNIT_K):
                    split()
                    counts["unit"].next()
                    if first:
                        root()
                    split(k_next)
                    counts["unit"].next()
                    act.wait_ge(evacuated[0], counts["ev0"].next())
                    nc.scalar.activation(gs[:, :], gs[:, :], ACT.Silu).then_inc(silu_made, 1)
                    counts["ev1"].next()
                def inner_hi(i):
                    act.wait_ge(act_made, counts["act"].next())
                    nc.scalar.activation(pair(act_hi, i), us[:, :], ACT.Copy).then_inc(act_hi_made, 1)
                inner(True)
                inner_hi(0)
                with rounds(act, FF_UNITS - 2, counts, unit=2, raw0=16, raw1=16, ev0=1, ev1=1, act=1) as i:
                    inner(False)
                    inner_hi(i + 1)
                inner(False, widths[0])
                inner_hi(FF_UNITS - 1)
                for d in range(D_PAIRS):
                    for n in range(3):
                        end = d == D_PAIRS - 1 and n == 2
                        if end and last:
                            with act.If(layer < DEPTH - 1):
                                split()
                        else:
                            split(UNIT_K if end else widths[(n + 1) % 3])
                        counts["unit"].next()
                    residual(layer, gain, d, d % 2)

            act.dma_start(x_in[:, 0:D], x[0, 0:P, :]).then_inc(x_loaded, 16)
            for t in range(1, TILES):
                act.dma_start(x_in[:, t * D:(t + 1) * D], x[0, t * P:(t + 1) * P, :]).then_inc(x_loaded, 16)
            split()
            act.wait_ge(side_done[1], counts["sd1"].next())
            nc.scalar.activation(table[:, 0:N_VEC], side[1][:, 0:N_VEC], ACT.Copy).then_inc(side_evacuated[1], 1)
            act.wait_ge(side_evacuated[1], 2)
            for d in range(D_PAIRS):
                residual(0, T_FFN1, d, d % 2, (us, gs)[d % 2])

            with rounds(act, DEPTH, counts, unit=UNITS_PER_LAYER, raw0=8 * UNITS_PER_LAYER + 16 * 2,
                        raw1=8 * UNITS_PER_LAYER + 16 * 3, ev0=EV0, ev1=EV1, se0=5 + ATT, act=2 * FF_UNITS,
                        sd0=5 + ATT, sd1=3, ln=1, yb=2, neg=ATT, pT_written=ATT, head=ATT, merged=D_PAIRS) as layer:
                ffn(layer, layer * KD + T_MIX, False)

                act.dma_start(w_s[:, :].rearrange("p (g s) -> p g s", s=CHUNK),
                              b_w_s[bass.ds(layer, 1)].rearrange("a g t s -> t (a g) s")).then_inc(params_loaded, 16)
                act.dma_start(cw[:, :].rearrange("p (g s) -> p g s", s=P),
                              c_w[bass.ds(layer, 1)].rearrange("a g t s -> t (a g) s")).then_inc(params_loaded, 16)
                act.dma_start(bias_s[:, :], b_b_s[bass.ds(layer, 1)].rearrange("a g s -> (a g s)").partition_broadcast(P)).then_inc(params_loaded, 16)
                act.dma_start(ln_g[:, :], b_ln_g[bass.ds(layer, 1)].rearrange("a s -> (a s)").partition_broadcast(P)).then_inc(params_loaded, 16)
                act.dma_start(ln_b[:, :], b_ln_b[bass.ds(layer, 1)].rearrange("a s -> (a s)").partition_broadcast(P)).then_inc(params_loaded, 16)

                step()
                root(norm_cols)
                counts["ev0"].next()
                act.wait_ge(side_done[1], counts["sd1"].next())
                nc.scalar.activation(w_sT[:, :], side[1][:, 0:KB * P], ACT.Copy).then_inc(side_evacuated[1], 1)
                step()
                counts["ev1"].next()

                def pool_hi(s):
                    act.wait_ge(side_done[s], counts[f"sd{s}"].next())
                    if s == 0:
                        counts["se0"].next()
                    for c in range(2):
                        g = 2 * s + c
                        mm = nc.scalar.activation(yc_hi[:, g * S:(g + 1) * S], side[s][:, c * S:(c + 1) * S], ACT.Copy,
                                                  scale=table[:, bass.ds(T_CSCALE + layer * KB + g, 1)])
                    mm.then_inc(yc_hi_made, 1)

                for u in range(2):
                    step()
                    act.wait_ge(evacuated[u], counts[f"ev{u}"].next())
                    nc.scalar.activation(pair(ub, u), pair(ub, u), ACT.Gelu).then_inc(gelu_made, 1)
                    pool_hi(u)
                act.wait_ge(rstd_made, 2 + layer * 3)
                for u in range(2):
                    step()
                    act.wait_ge(unit_done, counts["unit"].now(2))
                    for t in range(TILES):
                        mm = nc.scalar.activation(vb[:, t * BW + u * UNIT_N:t * BW + (u + 1) * UNIT_N],
                                                  psum[u][:, t * UNIT_N:(t + 1) * UNIT_N], ACT.Gelu,
                                                  scale=norm_cols[:, t:t + 1])
                    mm.then_inc(evacuated[u], 1)
                    counts[f"ev{u}"].next()
                def gating_hi(s):
                    act.wait_ge(yb_made, counts["yb"].next())
                    nc.scalar.activation(pair(yb_hi, s), gs[:, :], ACT.Copy).then_inc(yb_hi_made, 1)

                act.wait_ge(ln_var_made, counts["ln"].next())
                nc.scalar.activation(ln_rs, ln_rs, ACT.Sqrt).then_inc(ln_std_made, 1)
                for u in range(GROUPS):
                    step(parts=1 if u < GROUPS - 1 else 2)
                    act.wait_ge(unit_done, counts["unit"].now(2))
                    for t in range(TILES):
                        mm = nc.scalar.activation(v[:, t * A_WIDTH + u * UNIT_N:t * A_WIDTH + (u + 1) * UNIT_N],
                                                  psum[u % 2][:, t * UNIT_N:(t + 1) * UNIT_N], ACT.Copy,
                                                  scale=norm_cols[:, TILES + t:TILES + t + 1])
                    mm.then_inc(evacuated[u % 2], 1)
                    counts[f"ev{u % 2}"].next()
                    if u == 2:
                        gating_hi(0)
                step(parts=2)
                counts["ev1"].next()
                gating_hi(1)
                step(n=P)
                counts["ev0"].next()
                step(n=P)
                step(parts=2)
                counts["ev1"].next()
                counts["sd0"].next(1 + ATT)
                counts["se0"].next(1 + ATT)
                counts["sd1"].next()

                def head_hi(n):
                    j, r = divmod(n, RES)
                    rows_ = slice((j % 2) * HEAD_DIM, (j % 2 + 1) * HEAD_DIM)
                    act.wait_ge(head_done, counts["head"].next())
                    dst = ya_hi[rows_, (j // 2) * S:(j // 2 + 1) * S].rearrange("p (i r) -> p r i", r=RES)[:, r, :]
                    nc.scalar.activation(dst, side[1][rows_, KEYS:KEYS + P],
                                         ACT.Copy).then_inc(ya_hi_made, 1)

                def sigmoids(g, s, col):
                    act.wait_ge(evacuated[s], counts[f"ev{s}"].next())
                    for c in range(2):
                        mm = nc.scalar.activation(gate[g][:, c * S:(c + 1) * S], gate[g][:, c * S:(c + 1) * S], ACT.Sigmoid,
                                                  bias=table[:, bass.ds(col + (g * KD + c), 1)])
                    mm.then_inc(gate_made, 1)

                bias_col = T_BGATE + layer * (3 * KD)
                next_unit = [dict(parts=2), dict(parts=2), {}, {}, {}, dict(k=KA)]
                for s in range(SLOTS):
                    m, third = divmod(s, 3)
                    if attended(s - 1) is not None:
                        head_hi(attended(s - 1))
                    if third == 0:
                        if m > 0:
                            counts["unit"].next()
                            if m - 1 < 3:
                                counts[f"ev{(m - 1) % 2}"].next()
                        split(**next_unit[m])
                    if third == 1 and m > 3:
                        sigmoids(m - 4, (m - 1) % 2, bias_col)
                    if attended(s) is not None:
                        act.wait_ge(pT_written, counts["pT_written"].next())
                        nc.scalar.activation(pT[:, :], side[1][:, 0:KEYS], ACT.Copy).then_inc(pT_made, 1)
                    if attended(s + 1) is not None:
                        n = attended(s + 1)
                        act.wait_ge(neg_max_made, counts["neg"].next())
                        nc.scalar.activation(p_tile[n % 2][:, :], p_tile[n % 2][:, :], ACT.Exp, bias=neg_max[:, n % 2:n % 2 + 1],
                                             accum_out=row_sum[:, n % 2:n % 2 + 1]).then_inc(exp_made, 1)
                head_hi(ATT - 1)
                counts["unit"].next()

                def project(d, col):
                    step(KB)
                    sigmoids(2, 1, col)
                    step(KB)
                    step()
                    counts["ev0"].next(2)
                    counts["ev1"].next()
                    act.wait_ge(merged_made, counts["merged"].next())
                    nc.scalar.activation(pair(m_hi, d), gate[0][:, :], ACT.Copy).then_inc(merged_hi_made, 1)

                project(0, bias_col)
                with rounds(act, D_PAIRS - 1, counts, unit=6, raw0=48, raw1=48, ev0=3, ev1=3, merged=1) as i:
                    col = bias_col + i * 2 + 2
                    for g in range(3):
                        step(KA if g == 2 else UNIT_K)
                        if g < 2:
                            sigmoids(g, 1 - g % 2, col)
                    project(i + 1, col)
                with rounds(act, D_PAIRS // 2, counts, unit=2, raw0=16, raw1=16, ev0=1, ev1=1) as half:
                    for d in range(2):
                        step()
                        residual(layer, layer * KD + T_FFN2, half * 2 + d, d)
                ffn(layer, layer * KD + (T_FFN1 + KD), True)

            act.wait_ge(side_evacuated[0], counts["se0"].next())
            nc.scalar.activation(norm_cols, norm_cols, ACT.Sqrt).then_inc(std_made, 1)

        @block.vector
        def _(dve):
            counts = {k: Count() for k in ("unit", "hi", "step", "h_hi", "sq", "acc", "side0", "side1", "std", "rstd",
                                           "silu", "act_hi", "gelu", "ln_std", "yc_hi", "yb_hi", "exp",
                                           "head", "gate", "merged", "pooled", "y")}
            counts |= {k: Count(1) for k in ("ev0", "ev1", "se0", "se1")}
            slot = [0]

            def side_out(s, ins):
                ins.then_inc(side_evacuated[s], 1)
                return counts[f"se{s}"].next()

            def chain(ins):
                ins.then_inc(dve_step, 1)
                dve.wait_ge(dve_step, counts["step"].next())

            def split(k=UNIT_K, n=UNIT_N):
                s = slot[0]
                slot[0] = 1 - s
                dve.wait_ge(hi_made, counts["hi"].next())
                a = slice(0, k * n)
                nc.vector.tensor_tensor(w_lo[s][:, a], raw[s][:, a], w_hi[s][:, a].bitcast(F32),
                                        ALU.subtract).then_inc(split_made, 1)

            def step(k=UNIT_K, n=UNIT_N):
                split(k, n)
                done()

            def done():
                dve.wait_ge(unit_done, counts["unit"].next() + 2)

            def evac(s, ins):
                ins.then_inc(evacuated[s], 1)
                return counts[f"ev{s}"].next()

            rstd2 = rstd[:, :].unsqueeze(1).broadcast_to([P, 2, S])

            def two(t):
                return t.rearrange("p (c s) -> p c s", s=S)

            def scaled(dst, s):
                return nc.vector.tensor_tensor(dst, two(psum[s][:, :]), rstd2, ALU.mult)

            def residual(scale, gain, d, s):
                take(scale, d, s)
                prepare(gain, d)

            def take(scale, d, s):
                x_ = pair(xT, d)
                if scale is None:
                    v_ = evac(s, nc.vector.tensor_copy(x_, psum[s][:, :]))
                else:
                    v_ = evac(s, nc.vector.scalar_tensor_tensor(x_, psum[s][:, :], scale, x_, ALU.mult, ALU.add))
                dve.wait_ge(evacuated[s], v_)

            def prepare(gain, d, sq=us):
                dve.wait_ge(h_hi_made, counts["h_hi"].next())
                for c in range(2):
                    a = bass.ds(d * (2 * S) + c * S, S)
                    i_ = nc.vector.scalar_tensor_tensor(h_lo[:, a], xT[:, a], table[:, bass.ds(gain + 2 * d + c, 1)],
                                                        h_hi[:, a].bitcast(F32), ALU.mult, ALU.subtract)
                i_.then_inc(h_ready, 1)
                dve.wait_ge(sq_made, counts["sq"].next())
                dve.wait_ge(acc_ready, counts["acc"].now())
                nc.vector.tensor_tensor(acc[:, :], acc[:, :], sq[:, :], ALU.add).then_inc(acc_ready, 1)
                counts["acc"].next()

            def clear_acc():
                nc.vector.memset(acc[:, :], 0.0).then_inc(acc_ready, 1)
                counts["acc"].next()

            def inverse_root(by_token):
                dve.wait_ge(side_done[0], counts["side0"].next())
                if by_token:
                    nc.vector.tensor_scalar(norm_cols, side[0][:, S:S + 2 * TILES], 1.0 / D, EPS, ALU.mult, ALU.add)
                side_out(0, nc.vector.tensor_scalar(rstd[:, :], side[0][:, 0:S], 1.0 / D, EPS, ALU.mult, ALU.add))
                dve.wait_ge(std_made, counts["std"].next())
                if by_token:
                    nc.vector.reciprocal(norm_cols, norm_cols)
                nc.vector.reciprocal(rstd[:, :], rstd[:, :]).then_inc(rstd_made, 1)
                dve.wait_ge(rstd_made, counts["rstd"].next())

            def ffn(layer, gain, last):
                def inner(i, first=False, k_next=UNIT_K):
                    split()
                    if first:
                        inverse_root(False)
                    done()
                    evac(0, scaled(two(gs[:, :]), 0))
                    step(k_next)
                    v_ = evac(1, scaled(two(us[:, :]), 1))
                    dve.wait_ge(evacuated[1], v_)
                    dve.wait_ge(silu_made, counts["silu"].next())
                    nc.vector.tensor_tensor(us[:, :], us[:, :], gs[:, :], ALU.mult).then_inc(act_made, 1)
                    dve.wait_ge(act_hi_made, counts["act_hi"].next())
                    nc.vector.tensor_tensor(pair(act_lo, i), us[:, :], pair(act_hi, i).bitcast(F32),
                                            ALU.subtract).then_inc(act_ready, 1)
                inner(0, True)
                with rounds(dve, FF_UNITS - 2, counts, unit=2, hi=2, ev0=1, ev1=1, silu=1, act_hi=1) as i:
                    inner(i + 1)
                inner(FF_UNITS - 1, k_next=DOWN_K[0][1])
                clear_acc()
                widths = [k1 - k0 for k0, k1 in DOWN_K]
                for d in range(D_PAIRS):
                    for n in range(3):
                        end = d == D_PAIRS - 1 and n == 2
                        if end and last:
                            with dve.If(layer < DEPTH - 1):
                                split()
                        else:
                            split(UNIT_K if end else widths[(n + 1) % 3])
                        if n == 2:
                            done()
                        else:
                            counts["unit"].next()
                    residual(0.5, gain, d, d % 2)

            handed = 100
            for s_, n in ((evacuated[0], 1), (evacuated[1], 1), (side_evacuated[0], 1), (side_evacuated[1], 1),
                          (split_made, 2), (unit_done, 2), (head_made, 1)):
                for _ in range(n):
                    nc.vector.memset(small[:, handed:handed + 1], 0.0).then_inc(s_, 1)
                    handed += 1
            for i in range(PAD):
                nc.vector.memset(inv_count[:, i:i + 1], 1.0 / (i + 1))
            clear_acc()

            dve.wait_ge(side_evacuated[1], counts["se1"].next())
            counts["side1"].next()
            split()
            for d in range(D_PAIRS + 1):
                if d < D_PAIRS:
                    dve.wait_ge(turned, d + 1)
                    take(None, d, d % 2)
                if d > 0:
                    prepare(T_FFN1, d - 1, (us, gs)[(d - 1) % 2])

            chained = sum(w.bit_length() for w in POOL_WINDOWS) + 5 + D_PAIRS + ATT
            with rounds(dve, DEPTH, counts, unit=UNITS_PER_LAYER, hi=UNITS_PER_LAYER, ev0=EV0, ev1=EV1, step=chained,
                        h_hi=12, sq=12, acc=15, side0=5 + ATT, side1=3, se0=5 + ATT, se1=3, std=3, rstd=3, silu=2 * FF_UNITS,
                        act_hi=2 * FF_UNITS, gelu=2, ln_std=1, yc_hi=2, yb_hi=2, y=2, pooled=KB, exp=ATT,
                        head=ATT, gate=3 * D_PAIRS, merged=D_PAIRS) as layer:
                ffn(layer, layer * KD + T_MIX, False)

                def pool_sums(g):
                    w = POOL_WINDOWS[g]
                    c = c_pad[:, g * CP:(g + 1) * CP]
                    cur, shift, b = c, 1, 0
                    while shift < w:
                        nxt = sums[b]
                        chain(nc.vector.tensor_tensor(nxt[:, PAD:CP], cur[:, PAD:CP], cur[:, PAD - shift:CP - shift], ALU.add))
                        cur, shift, b = nxt, 2 * shift, 1 - b
                    chain(nc.vector.tensor_tensor(pool_head[:, 0:w - 1], cur[:, PAD:PAD + w - 1], inv_count[:, 0:w - 1], ALU.mult))
                    nc.vector.tensor_tensor(c[:, PAD:PAD + w - 1], pool_head[:, 0:w - 1], c[:, PAD:PAD + w - 1],
                                            ALU.subtract)
                    nc.vector.scalar_tensor_tensor(c[:, PAD + w - 1:CP], cur[:, PAD + w - 1:CP], 1.0 / w,
                                                   c[:, PAD + w - 1:CP], ALU.mult, ALU.subtract).then_inc(pooled, 1)
                    dve.wait_ge(pooled, counts["pooled"].next())

                def yc_lo_part(s):
                    dve.wait_ge(yc_hi_made, counts["yc_hi"].next())
                    for c in range(2):
                        g = 2 * s + c
                        i_ = nc.vector.scalar_tensor_tensor(yc_lo[:, g * S:(g + 1) * S], side[s][:, c * S:(c + 1) * S],
                                                            table[:, bass.ds(T_CSCALE + layer * KB + g, 1)],
                                                            yc_hi[:, g * S:(g + 1) * S].bitcast(F32), ALU.mult, ALU.subtract)
                    side_out(s, i_)

                for u in range(2):
                    split()
                    if u == 0:
                        inverse_root(True)
                        for i in range(4):
                            nc.vector.memset(c_pad[:, i * CP:i * CP + PAD], 0.0)
                        for s in range(2):
                            nc.vector.memset(sums[s][:, 0:PAD], 0.0)
                    done()
                    c2 = c_pad[:, 2 * u * CP:2 * (u + 1) * CP].rearrange("p (c s) -> p c s", s=CP)[:, :, PAD:CP]
                    v_ = evac(u, scaled(c2, u))
                    dve.wait_ge(evacuated[u], v_)
                    for c in range(2):
                        pool_sums(2 * u + c)
                for u in range(2):
                    step()
                    evac(u, scaled(two(pair(ub, u)), u))
                    if u == 1:
                        counts["side1"].next()
                        counts["se1"].next()
                    yc_lo_part(u)
                    counts[f"side{u}"].next()
                for u in range(2):
                    split()
                    counts["unit"].next()
                    counts[f"ev{u}"].next()
                for u in range(2):
                    dve.wait_ge(evacuated[u], counts[f"ev{u}"].now())
                for t in range(TILES):
                    i_ = nc.vector.bn_stats(ln_stats[:, 6 * t:6 * t + 6], vb[:, t * BW:(t + 1) * BW])
                chain(i_)
                nc.vector.memset(small[:, 126:127], 0.0)
                for t in range(TILES):
                    i_ = nc.vector.bn_aggr(ln_mv[:, 2 * t:2 * t + 2], ln_stats[:, 6 * t:6 * t + 6])
                chain(i_)
                var = ln_mv.rearrange("p (t c) -> p t c", c=2)[:, :, 1]
                nc.vector.tensor_scalar(ln_rs, var, EPS, None, ALU.add).then_inc(ln_var_made, 1)
                dve.wait_ge(ln_std_made, counts["ln_std"].next())
                chain(nc.vector.reciprocal(ln_rs, ln_rs))
                for t in range(TILES):
                    i_ = nc.vector.tensor_scalar(vb[:, t * BW:(t + 1) * BW], vb[:, t * BW:(t + 1) * BW],
                                                 ln_mv[:, 2 * t:2 * t + 1], ln_rs[:, t:t + 1], ALU.subtract, ALU.mult)
                chain(i_)
                split()
                vb4 = vb[:, :].rearrange("p (t c) -> p t c", c=BW)
                dve.wait_ge(params_loaded, 16 * 5 + layer * (16 * 5))
                chain(nc.vector.tensor_tensor(vb4, vb4, ln_g[:, :].unsqueeze(1).broadcast_to([P, TILES, BW]), ALU.mult))
                nc.vector.tensor_tensor(vb4, vb4, ln_b[:, :].unsqueeze(1).broadcast_to([P, TILES, BW]),
                                        ALU.add).then_inc(vb_ready, 1)

                def gating(s):
                    dve.wait_ge(side_done[s], counts[f"side{s}"].next())
                    if s == 0:
                        dve.wait_ge(gelu_made, counts["gelu"].next(2))
                    g4 = gs[:, :].rearrange("p (g b t) -> p g b t", g=2, t=CHUNK)
                    v_ = side_out(s, nc.vector.tensor_tensor(
                        g4, side[s][:, :].rearrange("p (g b t) -> p g b t", g=2, t=CHUNK),
                        bias_s[:, 2 * s * CHUNK:2 * (s + 1) * CHUNK].rearrange("p (g t) -> p g t", t=CHUNK)
                        .unsqueeze(2).broadcast_to([P, 2, TILES, CHUNK]), ALU.add))
                    dve.wait_ge(side_evacuated[s], v_)
                    nc.vector.tensor_tensor(gs[:, :], gs[:, :], pair(ub, s), ALU.mult).then_inc(yb_made, 1)
                    dve.wait_ge(yb_hi_made, counts["yb_hi"].next())
                    nc.vector.tensor_tensor(pair(yb_lo, s), gs[:, :], pair(yb_hi, s).bitcast(F32),
                                            ALU.subtract).then_inc(y_ready, 1)
                    dve.wait_ge(y_ready, counts["y"].next())
                for u in range(GROUPS):
                    if u > 0:
                        split()
                    counts["unit"].next()
                    counts[f"ev{u % 2}"].next()
                    if u == 2:
                        gating(0)
                rstd_i = rstd[:, :].rearrange("p (i r) -> p i r", r=RES)

                def take_qk(jp, chunk, s, c):
                    d_ = qk[jp][:, chunk * S:(chunk + 1) * S].rearrange("p (r i) -> p i r", r=RES)
                    s_ = psum[s][:, c * S:(c + 1) * S].rearrange("p (i r) -> p i r", r=RES)
                    return nc.vector.scalar_tensor_tensor(d_, s_, HEAD_DIM ** -0.5 if chunk < GROUPS else 1.0, rstd_i,
                                                          ALU.mult, ALU.mult)

                step()
                take_qk(0, 0, 1, 0)
                evac(1, take_qk(0, 1, 1, 1))
                gating(1)
                step(n=P)
                take_qk(0, 2, 0, 0)
                evac(0, take_qk(0, 3, 0, 1))
                step(n=P)
                take_qk(0, 4, 1, 0)
                step()
                evac(1, take_qk(0, 5, 1, 1))

                def head_lo(n):
                    j, r = divmod(n, RES)
                    rows_ = slice((j % 2) * HEAD_DIM, (j % 2 + 1) * HEAD_DIM)
                    dve.wait_ge(ya_hi_made, counts["head"].next())
                    a = slice((j // 2) * S, (j // 2 + 1) * S)
                    nc.vector.tensor_tensor(ya_lo[rows_, a].rearrange("p (i r) -> p r i", r=RES)[:, r, :],
                                            side[1][rows_, KEYS:KEYS + P],
                                            ya_hi[rows_, a].rearrange("p (i r) -> p r i", r=RES)[:, r, :].bitcast(F32),
                                            ALU.subtract).then_inc(head_made, 1)

                def score_max(n):
                    dve.wait_ge(side_done[0], counts["side0"].next())
                    b = slice(n % 2, n % 2 + 1)
                    r = n % RES
                    nc.vector.memset(small[:, 126:127], 0.0)
                    v_ = side_out(0, nc.vector.tensor_tensor_reduce(
                        p_tile[n % 2][:, :], side[0][:, 0:KEYS], masks[:, r * KEYS:(r + 1) * KEYS],
                        1.0, 3 * MASKED, ALU.add, ALU.max, row_max[:, b]))
                    dve.wait_ge(side_evacuated[0], v_)
                    nc.vector.tensor_scalar(neg_max[:, b], row_max[:, b], -1.0, None, ALU.mult).then_inc(neg_max_made, 1)

                def normalise(n):
                    b = slice(n % 2, n % 2 + 1)
                    dve.wait_ge(exp_made, counts["exp"].next())
                    chain(nc.vector.reciprocal(row_inv[:, b], row_sum[:, b]))
                    nc.vector.tensor_scalar(p_tile[n % 2][:, :], p_tile[n % 2][:, :], row_inv[:, b], None,
                                            ALU.mult).then_inc(p_made, 1)

                def take_gate(g, s):
                    evac(s, scaled(two(gate[g][:, :]), s))

                dve.wait_ge(mask_step, MASK_STEPS)
                def take_unit(m):
                    done()
                    if m < 3:
                        a = QK_UNITS[m]
                        take_qk(1, a[0], m % 2, 0)
                        evac(m % 2, take_qk(1, a[1], m % 2, 1))
                    else:
                        take_gate(m - 3, m % 2)

                for s in range(SLOTS):
                    m, third = divmod(s, 3)
                    if attended(s - 1) is not None:
                        head_lo(attended(s - 1))
                    if third == 0 and m > 0 and attended(s) is None:
                        take_unit(m - 1)
                    if attended(s + 1) is not None:
                        score_max(attended(s + 1))
                    if third == 0:
                        split(UNIT_K if m < 5 else KA)
                        if m > 0 and attended(s) is not None:
                            take_unit(m - 1)
                    if attended(s + 1) is not None:
                        normalise(attended(s + 1))
                head_lo(ATT - 1)
                done()
                take_gate(2, 1)

                def project(d):
                    step(KB)
                    dve.wait_ge(gate_made, counts["gate"].next())
                    evac(0, nc.vector.tensor_tensor(gate[0][:, :], gate[0][:, :], psum[0][:, :], ALU.mult))
                    step(KB)
                    dve.wait_ge(gate_made, counts["gate"].next())
                    v_ = evac(1, nc.vector.tensor_tensor(gate[1][:, :], gate[1][:, :], psum[1][:, :], ALU.mult))
                    dve.wait_ge(evacuated[1], v_)
                    chain(nc.vector.tensor_tensor(gate[0][:, :], gate[0][:, :], gate[1][:, :], ALU.add))
                    step()
                    dve.wait_ge(gate_made, counts["gate"].next())
                    v_ = evac(0, nc.vector.tensor_tensor(gate[2][:, :], gate[2][:, :], psum[0][:, :], ALU.mult))
                    dve.wait_ge(evacuated[0], v_)
                    nc.vector.tensor_tensor(gate[0][:, :], gate[0][:, :], gate[2][:, :], ALU.add).then_inc(merged_made, 1)
                    dve.wait_ge(merged_hi_made, counts["merged"].next())
                    nc.vector.tensor_tensor(pair(m_lo, d), gate[0][:, :], pair(m_hi, d).bitcast(F32),
                                            ALU.subtract).then_inc(merged_ready, 1)

                project(0)
                with rounds(dve, D_PAIRS - 1, counts, unit=6, hi=6, ev0=3, ev1=3, step=1, gate=3, merged=1) as i:
                    for g in range(3):
                        step(KA if g == 2 else UNIT_K)
                        if g == 0:
                            dve.wait_ge(merged_ready, counts["merged"].now())
                        take_gate(g, 1 - g % 2)
                    project(i + 1)
                clear_acc()
                with rounds(dve, D_PAIRS // 2, counts, unit=2, hi=2, ev0=1, ev1=1, h_hi=2, sq=2, acc=2) as half:
                    for d in range(2):
                        step()
                        residual(1.0, layer * KD + T_FFN2, half * 2 + d, d)
                ffn(layer, layer * KD + (T_FFN1 + KD), True)

            dve.wait_ge(side_done[0], counts["side0"].next())
            nc.vector.tensor_scalar(norm_cols, side[0][:, 0:2 * TILES], 1.0 / D, EPS, ALU.mult, ALU.add).then_inc(side_evacuated[0], 1)
            dve.wait_ge(std_made, counts["std"].next())
            chain(nc.vector.reciprocal(norm_cols, norm_cols))
            dve.wait_ge(gains_loaded, 16)
            for t in range(TILES):
                dve.wait_ge(turned, D_PAIRS + t + 1)
                nc.vector.scalar_tensor_tensor(x_out[:, t * D:(t + 1) * D], (psum[0], psum[1], side[1], psum[0])[t][:, :], norm_cols[:, t:t + 1],
                                               gain_rows[:, :], ALU.mult, ALU.mult).then_inc(out_made, 1)



_INS = ["x", "ffn1_norm", "ffn1_w_gate", "ffn1_w_up", "ffn1_w_down", "mix_norm", "w_in", "b_gate", "b_ln_g",
        "b_ln_b", "b_w_s", "b_b_s", "c_w", "c_scale", "w_proj_a", "w_proj_b", "w_proj_c", "w_out", "ffn2_norm",
        "ffn2_w_gate", "ffn2_w_up", "ffn2_w_down", "final_norm"]


def kernel(**inputs):
    import numpy as _np
    import concourse.bacc as _bacc
    from concourse import mybir as _mybir
    from concourse.bass_utils import run_bass_kernel_spmd as _run

    nc = _bacc.Bacc("TRN2", target_bir_lowering=False, num_devices=1)
    arrays, args = {}, []
    for name in _INS:
        a = _np.ascontiguousarray(inputs[name])
        arrays[f"in_{name}_dram"] = a
        args.append(nc.dram_tensor(f"in_{name}_dram", a.shape, _mybir.dt.from_np(a.dtype), kind="ExternalInput").ap())
    shape = inputs["x"].shape
    out = nc.dram_tensor("out_0_dram", shape, _mybir.dt.float32, kind="ExternalOutput").ap()
    trunk(nc, *args, out)
    r = _run(nc, [arrays], core_ids=[0])
    return r.results[0]["out_0_dram"]
```
